# Optimizing a Trainium2 kernel written in Bass

```python
import math
import jax
import jax.numpy as jnp
from jax import lax
import numpy as np

D_MODEL = 1024
BATCH = 1
SEQ = 512
DEPTH = 2

GRID_W = 64
CTX_LEN = 256
N_BRANCH = 3
BRANCH_W = D_MODEL // 2
CONV_K = 31
DN_HEADS = 4
DN_HEAD_K = BRANCH_W // DN_HEADS
DN_HEAD_V = BRANCH_W // DN_HEADS
DN_CHUNK = 64
SHORT_K = 3
DA_HEADS = 4
DA_HEAD = BRANCH_W // (2 * DA_HEADS)
ROPE_BASE = 10000.0
Q_BLOCK = 128
RMS_EPS = 1e-6
LN_EPS = 1e-5
IN_WIDTHS = (BRANCH_W, BRANCH_W, BRANCH_W,
             BRANCH_W, BRANCH_W, BRANCH_W, BRANCH_W,
             2 * DN_HEADS, 2 * DN_HEADS,
             BRANCH_W, BRANCH_W, BRANCH_W, BRANCH_W,
             N_BRANCH * D_MODEL)
IN_SPLITS = tuple(sum(IN_WIDTHS[:i + 1]) for i in range(len(IN_WIDTHS) - 1))
N_IN = sum(IN_WIDTHS)

kernel_name = 'hybrid_conv_deltanet_diffattn_prefix_dit'

def rms_norm(x, gain):
    xf = x.astype(jnp.float32)
    y = xf * lax.rsqrt(jnp.mean(xf * xf, axis=-1, keepdims=True) + RMS_EPS)
    return (y * gain.astype(jnp.float32)).astype(x.dtype)

def layer_norm(x, gain, bias):
    xf = x.astype(jnp.float32)
    mu = jnp.mean(xf, axis=-1, keepdims=True)
    xc = xf - mu
    y = xc * lax.rsqrt(jnp.mean(xc * xc, axis=-1, keepdims=True) + LN_EPS)
    return (y * gain.astype(jnp.float32) + bias.astype(jnp.float32)).astype(x.dtype)

def l2_norm(x):
    xf = x.astype(jnp.float32)
    return xf * lax.rsqrt(jnp.sum(xf * xf, axis=-1, keepdims=True) + RMS_EPS)

def depthwise_conv(x, w):
    pad = w.shape[0] // 2
    return lax.conv_general_dilated(x, w[:, None, :].astype(x.dtype), window_strides=(1,),
                                    padding=[(pad, pad)], dimension_numbers=('NWC', 'WIO', 'NWC'),
                                    feature_group_count=x.shape[-1])

def axial_rope_tables(n_rows):
    n_freq = DA_HEAD // 4
    inv_freq = ROPE_BASE ** (-jnp.arange(n_freq, dtype=jnp.float32) / n_freq)
    row = jnp.repeat(jnp.arange(n_rows, dtype=jnp.float32), GRID_W)
    col = jnp.tile(jnp.arange(GRID_W, dtype=jnp.float32), n_rows)
    ang = jnp.concatenate([row[:, None] * inv_freq, col[:, None] * inv_freq], axis=-1)
    ang = jnp.concatenate([ang, ang], axis=-1)
    return jnp.cos(ang), jnp.sin(ang)

def apply_rope(x, cos, sin):
    xf = x.astype(jnp.float32)
    half = xf.shape[-1] // 2
    rot = jnp.concatenate([-xf[..., half:], xf[..., :half]], axis=-1)
    return (xf * cos[:, None, None, :] + rot * sin[:, None, None, :]).astype(x.dtype)

def chunk_gated_delta(q, k, v, g, beta, s0):
    B, T, H, dk = q.shape
    dv = v.shape[-1]
    C = DN_CHUNK
    n = T // C

    def to_chunks(t):
        return jnp.transpose(t.astype(jnp.float32).reshape(B, n, C, H, -1), (1, 0, 3, 2, 4))

    q = to_chunks(q) * (dk ** -0.5)
    k = to_chunks(k)
    v = to_chunks(v)
    g = jnp.cumsum(to_chunks(g[..., None])[..., 0], axis=-1)
    beta = to_chunks(beta[..., None])[..., 0]
    lower = jnp.tril(jnp.ones((C, C), dtype=bool))
    strict = jnp.tril(jnp.ones((C, C), dtype=bool), -1)
    decay = jnp.where(lower, jnp.exp(jnp.where(lower, g[..., :, None] - g[..., None, :], 0.0)), 0.0)
    k_beta = k * beta[..., None]
    a = jnp.where(strict, jnp.einsum('nbhik,nbhjk->nbhij', k_beta, k) * decay, 0.0) + jnp.eye(C, dtype=jnp.float32)
    rhs = jnp.concatenate([v * beta[..., None], k_beta * jnp.exp(g)[..., None]], axis=-1)
    sol = lax.linalg.triangular_solve(a, rhs, left_side=True, lower=True, unit_diagonal=True)
    u, w = sol[..., :dv], sol[..., dv:]

    def step(S, xs):
        qc, kc, uc, wc, gc, dc = xs
        v_new = uc - jnp.einsum('bhck,bhkv->bhcv', wc, S)
        intra = jnp.einsum('bhik,bhjk->bhij', qc, kc) * dc
        o = jnp.einsum('bhck,bhkv->bhcv', qc * jnp.exp(gc)[..., None], S) + jnp.einsum('bhij,bhjv->bhiv', intra, v_new)
        g_last = gc[..., -1:]
        S = S * jnp.exp(g_last)[..., None] + jnp.einsum('bhck,bhcv->bhkv', kc * jnp.exp(g_last - gc)[..., None], v_new)
        return S, o

    s_final, o = lax.scan(step, s0.astype(jnp.float32), (q, k, u, w, g, decay))
    o = jnp.transpose(o, (1, 0, 3, 2, 4)).reshape(B, T, H, dv)
    return o, s_final

def delta_bidir(q, k, v, g, beta, s0_fwd, s0_bwd):
    o_f, s_f = chunk_gated_delta(q, k, v, g[:, :, 0], beta[:, :, 0], s0_fwd)
    rev = lambda t: jnp.flip(t, axis=1)
    o_b, s_b = chunk_gated_delta(rev(q), rev(k), rev(v), rev(g[:, :, 1]), rev(beta[:, :, 1]), s0_bwd)
    return o_f + rev(o_b), s_f, s_b

def diff_softmax_attend(q, K, V, lam):
    s = jnp.einsum('bqhmd,bkhmd->bhmqk', q, K).astype(jnp.float32)
    p = jax.nn.softmax(s, axis=-1)
    att = p[:, :, 0] - lam * p[:, :, 1]
    return jnp.einsum('bhqk,bkhe->bqhe', att.astype(V.dtype), V)

def diff_attention_latent(q, k, v, k_ctx, v_ctx, lam):
    B, S, H, _, d = q.shape
    q = q * (d ** -0.5)
    K = jnp.concatenate([k, k_ctx], axis=1)
    V = jnp.concatenate([v, v_ctx], axis=1)
    nb = S // Q_BLOCK
    qb = jnp.moveaxis(q.reshape(B, nb, Q_BLOCK, H, 2, d), 1, 0)
    o = lax.map(lambda qi: diff_softmax_attend(qi, K, V, lam), qb)
    return jnp.moveaxis(o, 0, 1).reshape(B, S, H, 2 * d)

def conv_module(val, glu, z, conv_w, conv_b, ln_g, ln_b):
    a = val * jax.nn.sigmoid(glu)
    a = depthwise_conv(a, conv_w) + conv_b
    return jax.nn.silu(layer_norm(a, ln_g, ln_b)) * jax.nn.silu(z)

def merge_branches(ys, gate_logits, w_branch, w_out):
    y = jnp.stack(ys, axis=2)
    proj = jnp.einsum('btnw,nwd->btnd', y, w_branch)
    gates = jax.nn.sigmoid(gate_logits.reshape(gate_logits.shape[0], gate_logits.shape[1], N_BRANCH, D_MODEL))
    return jnp.sum(gates * proj, axis=2) @ w_out

def trunk_layer(x, ctx, c, c_ctx, cos, sin, layer_idx, update_ctx,
                w_ada, b_ada, norm_g, w_in, conv_w, conv_b, conv_ln_g, conv_ln_b,
                dn_conv_w, dn_a_log, dn_dt_bias, dn_norm_g,
                da_q_norm_g, da_k_norm_g, da_lambda, da_subln_g, w_branch, w_out):
    B, S, _ = x.shape
    L = ctx.shape[1]
    shift, scale, gate = jnp.split(jax.nn.silu(c) @ w_ada + b_ada, 3, axis=-1)
    shift_c, scale_c, gate_c = jnp.split(jax.nn.silu(c_ctx) @ w_ada + b_ada, 3, axis=-1)
    h = rms_norm(x, norm_g) * (1.0 + scale[:, None]) + shift[:, None]
    h_c = rms_norm(ctx, norm_g) * (1.0 + scale_c) + shift_c
    (conv_val, conv_glu, conv_z, dq, dk, dv, dz, dbeta, ddecay,
     aq, ak, av, az, mgate) = jnp.split(h @ w_in, IN_SPLITS, axis=-1)
    (conv_val_c, conv_glu_c, conv_z_c, dq_c, dk_c, dv_c, dz_c, dbeta_c, ddecay_c,
     aq_c, ak_c, av_c, az_c, mgate_c) = jnp.split(h_c @ w_in, IN_SPLITS, axis=-1)

    def delta_inputs(q, k, v, beta_logit, decay_logit):
        T = q.shape[1]
        qkv = jax.nn.silu(depthwise_conv(jnp.concatenate([q, k, v], axis=-1), dn_conv_w))
        q, k, v = jnp.split(qkv, 3, axis=-1)
        q = l2_norm(q.reshape(B, T, DN_HEADS, DN_HEAD_K))
        k = l2_norm(k.reshape(B, T, DN_HEADS, DN_HEAD_K))
        v = v.reshape(B, T, DN_HEADS, DN_HEAD_V)
        beta = jax.nn.sigmoid(beta_logit.astype(jnp.float32)).reshape(B, T, 2, DN_HEADS)
        g = -jnp.exp(dn_a_log.astype(jnp.float32)) * jax.nn.softplus(
            decay_logit.astype(jnp.float32).reshape(B, T, 2, DN_HEADS) + dn_dt_bias.astype(jnp.float32))
        return q, k, v, g, beta

    s_zero = jnp.zeros((B, DN_HEADS, DN_HEAD_K, DN_HEAD_V), jnp.float32)
    o_dn_c, s_fwd, s_bwd = delta_bidir(*delta_inputs(dq_c, dk_c, dv_c, dbeta_c, ddecay_c), s_zero, s_zero)
    o_dn, _, _ = delta_bidir(*delta_inputs(dq, dk, dv, dbeta, ddecay), s_fwd, s_bwd)

    def delta_out(o, z):
        T = o.shape[1]
        return rms_norm(o, dn_norm_g).reshape(B, T, BRANCH_W).astype(z.dtype) * jax.nn.silu(z)

    lam_init = 0.8 - 0.6 * math.exp(-0.3 * layer_idx)
    lam_f = da_lambda.astype(jnp.float32)
    lam = jnp.exp(jnp.sum(lam_f[0] * lam_f[1])) - jnp.exp(jnp.sum(lam_f[2] * lam_f[3])) + lam_init

    def qk_heads(t, gain):
        return rms_norm(t.reshape(B, t.shape[1], DA_HEADS, 2, DA_HEAD), gain)

    k_ctx = qk_heads(ak_c, da_k_norm_g)
    v_ctx = av_c.reshape(B, L, DA_HEADS, 2 * DA_HEAD)
    q_lat = apply_rope(qk_heads(aq, da_q_norm_g), cos, sin)
    k_lat = apply_rope(qk_heads(ak, da_k_norm_g), cos, sin)
    v_lat = av.reshape(B, S, DA_HEADS, 2 * DA_HEAD)
    o_da = diff_attention_latent(q_lat, k_lat, v_lat, k_ctx, v_ctx, lam)

    def diff_out(o, z):
        T = o.shape[1]
        return (rms_norm(o, da_subln_g) * (1.0 - lam_init)).reshape(B, T, BRANCH_W) * jax.nn.silu(z)

    y_conv = conv_module(conv_val, conv_glu, conv_z, conv_w, conv_b, conv_ln_g, conv_ln_b)
    ys = (y_conv, delta_out(o_dn, dz), diff_out(o_da, az))
    x_new = x + gate[:, None] * merge_branches(ys, mgate, w_branch, w_out)

    if update_ctx:
        o_da_c = diff_softmax_attend(qk_heads(aq_c, da_q_norm_g) * (DA_HEAD ** -0.5), k_ctx, v_ctx, lam)
        ys_c = (conv_module(conv_val_c, conv_glu_c, conv_z_c, conv_w, conv_b, conv_ln_g, conv_ln_b),
                delta_out(o_dn_c, dz_c), diff_out(o_da_c, az_c))
        ctx = ctx + gate_c * merge_branches(ys_c, mgate_c, w_branch, w_out)
    return x_new, ctx

def setup_inputs(seed: int = 0) -> dict:
    key = jax.random.key(seed)
    ks = jax.random.split(key, 24)
    f32 = jnp.float32
    nrm = lambda k, shape, s: jax.random.normal(k, shape, f32) * s
    dt = jnp.exp(jax.random.uniform(ks[11], (DEPTH, 2, DN_HEADS), f32, math.log(0.001), math.log(0.1)))
    return {
        'x': nrm(ks[0], (BATCH, SEQ, D_MODEL), 1.0),
        'c': nrm(ks[1], (BATCH, D_MODEL), 1.0),
        'ctx': nrm(ks[2], (BATCH, CTX_LEN, D_MODEL), 1.0),
        'c_ctx': nrm(ks[3], (D_MODEL,), 1.0),
        'w_ada': nrm(ks[4], (DEPTH, D_MODEL, 3 * D_MODEL), 0.5 * D_MODEL ** -0.5),
        'b_ada': nrm(ks[5], (DEPTH, 3 * D_MODEL), 0.01),
        'norm_g': 1.0 + nrm(ks[6], (DEPTH, D_MODEL), 0.02),
        'w_in': nrm(ks[7], (DEPTH, D_MODEL, N_IN), D_MODEL ** -0.5),
        'conv_w': nrm(ks[8], (DEPTH, CONV_K, BRANCH_W), CONV_K ** -0.5),
        'conv_b': nrm(ks[9], (DEPTH, BRANCH_W), 0.01),
        'conv_ln_g': 1.0 + nrm(ks[10], (DEPTH, BRANCH_W), 0.02),
        'conv_ln_b': nrm(ks[12], (DEPTH, BRANCH_W), 0.01),
        'dn_conv_w': nrm(ks[13], (DEPTH, SHORT_K, 3 * BRANCH_W), SHORT_K ** -0.5),
        'dn_a_log': jnp.log(jax.random.uniform(ks[14], (DEPTH, 2, DN_HEADS), f32, 1.0, 16.0)),
        'dn_dt_bias': dt + jnp.log(-jnp.expm1(-dt)),
        'dn_norm_g': 1.0 + nrm(ks[15], (DEPTH, DN_HEAD_V), 0.02),
        'da_q_norm_g': 1.0 + nrm(ks[16], (DEPTH, DA_HEAD), 0.02),
        'da_k_norm_g': 1.0 + nrm(ks[17], (DEPTH, DA_HEAD), 0.02),
        'da_lambda': nrm(ks[18], (DEPTH, 4, DA_HEAD), 0.1),
        'da_subln_g': 1.0 + nrm(ks[19], (DEPTH, 2 * DA_HEAD), 0.02),
        'w_branch': nrm(ks[20], (DEPTH, N_BRANCH, BRANCH_W, D_MODEL), BRANCH_W ** -0.5),
        'w_out': nrm(ks[21], (DEPTH, D_MODEL, D_MODEL), D_MODEL ** -0.5),
    }

def reference(x, c, ctx, c_ctx, w_ada, b_ada, norm_g, w_in, conv_w, conv_b, conv_ln_g, conv_ln_b,
              dn_conv_w, dn_a_log, dn_dt_bias, dn_norm_g, da_q_norm_g, da_k_norm_g, da_lambda,
              da_subln_g, w_branch, w_out):
    n_rows = x.shape[1] // GRID_W
    cos, sin = axial_rope_tables(n_rows)
    for layer in range(DEPTH):
        x, ctx = trunk_layer(x, ctx, c, c_ctx, cos, sin, layer, layer < DEPTH - 1,
                             w_ada[layer], b_ada[layer], norm_g[layer], w_in[layer],
                             conv_w[layer], conv_b[layer], conv_ln_g[layer], conv_ln_b[layer],
                             dn_conv_w[layer], dn_a_log[layer], dn_dt_bias[layer], dn_norm_g[layer],
                             da_q_norm_g[layer], da_k_norm_g[layer], da_lambda[layer],
                             da_subln_g[layer], w_branch[layer], w_out[layer])
    return x


_drawn_inputs = setup_inputs


def setup_inputs(seed=0):
    import zlib

    import numpy as np

    out = dict(_drawn_inputs(seed))
    spreads = {}
    factors = {'b_ada': 5.97,
     'norm_g': 8.0,
     'conv_b': 8.0,
     'conv_ln_g': 8.0,
     'conv_ln_b': 8.0,
     'dn_norm_g': 8.0,
     'da_q_norm_g': 8.0,
     'da_k_norm_g': 8.0,
     'da_lambda': 4.456,
     'da_subln_g': 8.0}
    for name, (base, spread) in spreads.items():
        noise = np.random.default_rng([zlib.crc32(name.encode()), seed]).standard_normal(out[name].shape)
        drawn = base * np.exp(spread * noise) if base else spread * noise
        out[name] = jnp.asarray(drawn.astype(out[name].dtype))
    for name, factor in factors.items():
        out[name] = (out[name] * factor).astype(out[name].dtype)
    return out
```

```python
import math
from contextlib import ExitStack

import numpy as np

import concourse.bass as bass
from concourse import mybir

F32 = mybir.dt.float32
F32R = mybir.dt.float32r
ACT = mybir.ActivationFunctionType
ALU = mybir.AluOpType
AX_X = mybir.AxisListType.X

P = 128
D = 1024
KT = D // P
BW = 512
NT = BW // P
SEQ, CTX = 512, 256
TOK = SEQ + CTX
NC = TOK // P
DEPTH = 2
CK = 31
HALO = CK // 2
PADW = HALO + SEQ + HALO + CTX + HALO
ACCW = SEQ + HALO + CTX
LEVELS = 7
ORDER = ((4, 5, 0, 1, 2, 3), (5, 4, 3, 2, 1, 0))
RMS_EPS, LN_EPS = 1e-6, 1e-5
V_BADA, V_NG, V_CB, V_LG, V_LB = 0, 24, 32, 36, 40
V_CW = 44
V_DW = V_CW + NT * CK
V_DNG = V_DW + 3 * NT * 3
V_QG, V_KG, V_SUB, V_DT, V_AL = (V_DNG + i for i in range(1, 6))
NV = V_AL + 1
C_ID, C_BLK, C_ROT, C_NEG, C_MASK = 0, 128, 256, 384, 640
NCON = C_MASK + 2 * LEVELS * P


def ntok(l, kind):
    return TOK if l == 0 or kind in ("dk", "dv", "gb", "ak", "av") else SEQ


def segs(n):
    return [(0, SEQ), (SEQ, TOK)] if n == TOK else [(0, n)]


def schedule():
    out = [("ada", 0, g) for g in range(3)]
    for l in range(DEPTH):
        out += [("norm", l), ("gb", l)]
        for h in range(NT):
            out += [("dqkv", l, h, k) for k in ("dk", "dv", "dq")]
            if h % 2:
                out += [("dnorm", l, hh, k) for hh in (h - 1, h) for k in ("dk", "dq")]
        for s in range(NC):
            if l == 0 and s in (0, 2, 4):
                out.append(("ada", 1, s // 2))
            out += [("prep", l, s), ("scan", l, s)]
        out += [("dout", l, h) for h in range(NT)]
        out += [("glu", l, t) for t in range(NT)]
        out += [("mix", l, 1, p) for p in range(4)]
        out += [("ln", l)]
        out += [("z", l, t) for t in range(NT)]
        out += [("mix", l, 0, 0), ("qkv", l, 0), ("mix", l, 0, 1), ("mix", l, 0, 2), ("qkv", l, 1),
                ("att", l, 0), ("mix", l, 0, 3), ("aout", l, 0), ("qkv", l, 2), ("att", l, 1), ("aout", l, 1),
                ("qkv", l, 3), ("att", l, 2), ("aout", l, 2), ("att", l, 3), ("aout", l, 3)]
        out += [("mix", l, 2, p) for p in range(4)]
        out += [("out", l)]
    return out


def units_of(item):
    k, l = item[0], item[1]
    if k == "ada":
        return [("ada", l, 8 * item[2] + i) for i in range(8)]
    if k == "gb":
        return [("gb", l, 0)]
    if k == "dqkv":
        return [(item[3], l, item[2])]
    if k == "dout":
        return [("dz", l, item[2])]
    if k == "glu":
        return [("val", l, item[2]), ("glu", l, item[2])]
    if k == "z":
        return [("cz", l, item[2])]
    if k == "mix":
        n, p = item[2], item[3]
        return [("gate%d" % n, l, 2 * p), ("gate%d" % n, l, 2 * p + 1), ("branch%d" % n, l, p)]
    if k == "qkv":
        return [("aq", l, item[2]), ("ak", l, item[2]), ("av", l, item[2])]
    if k == "aout":
        return [("az", l, item[2])]
    if k == "out":
        return [("wout", l, d) for d in range(KT)]
    return []


ITEMS = schedule()
UNITS = [u for it in ITEMS for u in units_of(it)]
WIDX = {u: i for i, u in enumerate(UNITS)}
IN_COL = {"val": 0, "glu": 512, "cz": 1024, "dq": 1536, "dk": 2048, "dv": 2560, "dz": 3072, "gb": 3584,
          "aq": 3600, "ak": 4112, "av": 4624, "az": 5136, "gate0": 5648, "gate1": 6672, "gate2": 7696}


def build(nc, wstream, xT, cT, vec, lamr, con, rope, outT, steps):
    first_pass = not steps
    got = {}
    with ExitStack() as ctx:
        base = (nc.sbuf_base + 63) // 64 * 64
        pos = [base]

        def at(name, shape, dt=F32, off=None):
            n = 4 * int(np.prod(shape[1:]))
            if off is None:
                off = pos[0]
                pos[0] += (n + 31) // 32 * 32
            return nc.alloc_sbuf_tensor_at(name, shape, dt, offset=off)

        stages = ["start"] + sorted({it[0] for it in ITEMS})
        names = ["%s_%s" % (e, k) for e in ("pe", "act", "dve", "pool") for k in stages]
        names += ["w_high", "w_low", "raw0", "raw1", "raw2", "small_in", "x_in", "x_out", "rope_in"]
        sem = {n: ctx.enter_context(nc.semaphore(n)) for n in names}
        count = {n: 0 for n in sem}
        stage = ["start"]

        def tick(name, *key, by=1):
            name = {"hi": "w_high", "lo": "w_low"}.get(key[0], name)
            if name not in sem:
                name += "_" + stage[0]
            count[name] += by
            got[key] = (name, count[name])
            return sem[name], by

        def done(*key):
            assert first_pass or key in steps, key
            name, value = steps.get(key, ("x_in", 1))
            return sem[name], value

        hH = at("hH", [P, KT, TOK], F32R)
        hL = at("hL", [P, KT, TOK], F32R)
        raw = [at("raw%d" % i, [P, 1024]) for i in range(3)]
        wH = [at("wH%d" % i, [P, 1024], F32R) for i in range(3)]
        wL = [at("wL%d" % i, [P, 1024], F32R) for i in range(3)]
        cons = at("cons", [P, NCON])
        ones = at("ones", [P, P])
        vecs = at("vecs", [P, DEPTH, NV])
        csb = at("csb", [P, KT, 2])
        cs32 = at("cs32", [P, KT, 2])
        csH = at("csH", [P, KT, 2], F32R)
        csL = at("csL", [P, KT, 2], F32R)
        ada = at("ada", [P, DEPTH, 24, 2])
        gs = at("gs", [P, DEPTH, KT, 2])
        misc = at("misc", [P, 64])
        lam_dot = at("lam_dot", [P, DEPTH, 2])
        lam_exp = at("lam_exp", [P, DEPTH, 2])
        gcol = at("gcol", [P, 2, NC, 16])
        bcol = at("bcol", [P, NC, 16])
        stat = at("stat", [P, 2, 8])
        c1 = at("c1", [P, 2])
        lastc = at("lastc", [P, 2, 2, NT])
        eps = misc[:, 0:1]
        lneps = misc[:, 1:2]
        nega = misc[:, 2:4]
        nlam = misc[:, 4:6]
        qg8 = misc[:, 6:8]
        sub1 = misc[:, 8:10]
        pos[0] = (pos[0] + 63) // 64 * 64
        A0 = pos[0]
        AEND = A0 + (nc.sbuf_usable_end - A0) // 32 * 32
        ident = cons[:, C_ID:C_ID + P]
        blk = cons[:, C_BLK:C_BLK + P]
        rot = cons[:, C_ROT:C_ROT + P]

        def neg(d):
            return cons[:, C_NEG + d * P:C_NEG + (d + 1) * P]

        def mask(d, lv):
            o = C_MASK + (d * LEVELS + lv) * P
            return cons[:, o:o + P]

        T3 = 4 * TOK
        def arena(name, shape, off, dt=F32):
            assert A0 + off + 4 * int(np.prod(shape[1:])) <= AEND, (name, A0 + off, AEND)
            return at(name, shape, dt, A0 + off)

        qT = arena("qT", [P, NT, TOK], 0)
        kT = arena("kT", [P, NT, TOK], 4 * T3)
        Ktm = arena("Ktm", [P, NC, NT, P], 8 * T3)
        Vtm = arena("Vtm", [P, NC, NT, P], 12 * T3)
        oT = arena("oT", [P, NT, TOK], 16 * T3)
        B0 = 20 * T3
        names = ("Pm", "intra", "Kg", "Qg", "E", "EG", "AT", "X", "S", "vn", "vs")
        db = [{n: arena("%s%d" % (n, d), [P, NT, P], B0 + (d * len(names) + i) * 4 * BW)
               for i, n in enumerate(names)} for d in range(2)]
        GR = arena("GR", [48, TOK], B0 + 2 * len(names) * 4 * BW)
        pad3 = [arena("pad3_%d" % i, [P, TOK + 3], B0 + i * (T3 + 32)) for i in range(2)]
        c3 = [arena("c3_%d" % i, [P, TOK + 1], B0 + 2 * T3 + 64 + i * (T3 + 32)) for i in range(2)]
        vb = [arena("vb_%d" % i, [P, TOK], B0 + 4 * T3 + 128 + i * T3) for i in range(2)]
        sqd = [arena("sqd_%d" % i, [P, TOK], B0 + 6 * T3 + 128 + i * T3) for i in range(2)]
        rsd = [arena("rsd_%d" % i, [P, TOK], B0 + 8 * T3 + 128 + i * T3) for i in range(2)]
        gbt = [arena("gbt_%d" % i, [16, TOK], B0 + (10 + i) * T3 + 128) for i in range(4)]
        xs = arena("xs", [P, KT, TOK], 8 * T3)
        sqn = [arena("sqn_%d" % i, [P, TOK], (16 + i) * T3) for i in range(2)]
        rsn = arena("rsn", [P, TOK], 18 * T3)
        hn = [arena("hn_%d" % i, [P, TOK], (19 + i) * T3) for i in range(2)]
        mT = arena("mT", [P, KT, TOK], 0)
        yH = arena("yH", [P, NT, TOK], 8 * T3, F32R)
        yL = arena("yL", [P, NT, TOK], 12 * T3, F32R)
        CW = (4 * PADW * NT + 31) // 32 * 32
        GT = CW + 4 * ACCW * NT
        sg = [arena("sg%d" % i, [P, TOK], AEND - A0 - (3 - i) * T3) for i in range(2)]
        gm = arena("gm", [P, TOK], AEND - A0 - T3)
        do = [arena("do_%d" % i, [P, TOK], (20 + i) * T3) for i in range(10)]
        padc = arena("padc", [P, NT, PADW], 16 * T3)
        acc = arena("acc", [P, NT, ACCW], 16 * T3 + CW)
        CZ = (16 * T3 + GT + 31) // 32 * 32
        gl = [arena("gl_%d" % i, [P, TOK], CZ + i * T3) for i in range(2)]
        sqc = [arena("sqc_%d" % i, [P, ACCW], 16 * T3 + i * 3264) for i in range(2)]
        rsc = arena("rsc", [P, TOK], CZ)
        zt = [arena("zt_%d" % i, [P, TOK], 16 * T3 + i * T3) for i in range(4)]
        qh = [arena("qh_%d" % i, [P, TOK], (16 + i) * T3) for i in range(2)]
        kh = [arena("kh_%d" % i, [P, TOK], (18 + i) * T3) for i in range(2)]
        Va = [arena("Va_%d" % i, [P, NC, P], (20 + i) * T3) for i in range(2)]
        vr = arena("vr", [P, TOK], 22 * T3)
        at1 = [arena("at1_%d" % i, [P, TOK], (23 + i) * T3) for i in range(3)]
        Pa = [[arena("Pa_%d%d" % (i, m), [P, TOK], (26 + 2 * i + m) * T3) for m in range(2)] for i in range(2)]
        aT = [arena("aT_%d" % i, [P, NC, P], (30 + i) * T3) for i in range(2)]
        cs = arena("cs", [P, 2, SEQ], 32 * T3)
        lamt = arena("lamt", [P, DEPTH, 4, 64], 30 * T3)
        lamp = arena("lamp", [P, DEPTH, 2, 64], 31 * T3)

        xscr = nc.dram_tensor("x_between", (P, KT, TOK), F32, kind="Internal").ap()

        banks = ctx.enter_context(nc.psum_tensor("banks", [P, 8, 512], F32))
        bank_user = [None] * 8
        bank_next = [0]
        place = {}
        readers = {}

        def product(pe, key, width):
            n = 2 if width > 512 else 1
            b = bank_next[0]
            if n == 2 and b % 2:
                b += 1
            b %= 8
            bank_next[0] = (b + n) % 8
            for i in range(b, b + n):
                if bank_user[i] is not None and (i == b or bank_user[i] != bank_user[i - 1]):
                    last = 1 if ("read", bank_user[i], 1) in steps else 0
                    pe.wait_ge(*done("read", bank_user[i], last))
            for i in range(b, b + n):
                bank_user[i] = key
            place[key] = banks[:, b:b + n, :].rearrange("p b n -> p (b n)")
            return place[key]

        def tick_read(eng, key):
            r = readers.get(key, 0)
            readers[key] = r + 1
            return tick(eng, "read", key, r)

        def bc(ap, n=P):
            return ap.unsqueeze(2).to_broadcast([ap.shape[0], ap.shape[1], n])

        def v4(ap):
            return ap[:, 0:4 * P].rearrange("p (h c) -> p h c", h=4)

        def bh(ap):
            return ap.unsqueeze(1).to_broadcast([P, NT, P])

        mixes = [it for it in ITEMS if it[0] == "mix"]

        def lowh(l, t):
            dve = nc.vector
            for p, (a, b) in enumerate(segs(TOK)):
                dve.wait_ge(*done("hH", l, t, p))
                dve.scalar_tensor_tensor(hL[:, t, a:b], hn[t % 2][:, a:b], ada[:, l, t, p:p + 1],
                                              hH[:, t, a:b].bitcast(F32), ALU.add, ALU.subtract).then_inc(
                                                  *tick("dve", "h" if p else "hl0", l, t))

        def ocopy(l, h, qt):
            dve = nc.vector
            key = ("o", l, h, qt)
            dve.wait_ge(*done("pe", key))
            if qt == 0:
                dve.wait_ge(*done("rope", "ak", l, min(h + 1, 3)))
                if h:
                    dve.wait_ge(*done("ao", l, h - 1))
            ins = dve.tensor_copy(at1[2][:, qt * P:(qt + 1) * P], place[key][:, 0:P])
            ins.then_inc(*tick_read("dve", key))
            got[("ocopy", l, h, qt)] = got[("read", key, 0)]

        block = ctx.enter_context(nc.Block())

        @block.tensor
        def _(pe):
            stage[0] = "start"
            def dense(u, out, movH, movL, n, kts, col0=0, width=P):
                i = WIDX[u] % 3
                pe.wait_ge(*done("hi", u))
                pe.wait_ge(*done("lo", u))
                for kt in range(kts):
                    lo = kt * width + col0
                    H, L = wH[i][:, lo:lo + P], wL[i][:, lo:lo + P]
                    for j, (w, m) in enumerate(((H, movH), (H, movL), (L, movH))):
                        for a, b in n:
                            last = pe.matmul(out[:, a:b], w, m[:, kt, a:b], start=(kt == 0 and j == 0),
                                             stop=(kt == kts - 1 and j == 2))
                return last

            def unit(u, kind):
                out = product(pe, u, ntok(u[1], kind))
                pe.wait_ge(*done("h", u[1], KT - 1))
                last = dense(u, out, hH, hL, segs(ntok(u[1], kind)), KT)
                last.then_inc(*tick("pe", "pe", u))

            def allsum(key, stat_ap, tiles, n, dep, kt_n):
                out = product(pe, key, n)
                for t in range(kt_n):
                    pe.wait_ge(*done(*dep(t)))
                    for a, b in segs(n):
                        last = pe.matmul(out[:, a:b], stat_ap, tiles(t, a, b), start=(t == 0), stop=(t == kt_n - 1))
                    last.then_inc(*(tick("pe", "pe", key) if t == kt_n - 1 else tick("pe", "pe", key, t)))

            def turn(key, src, n, dep):
                out = product(pe, key, n)
                pe.wait_ge(*done(*dep))
                for c in range(n // P):
                    last = pe.transpose(out[:, c * P:(c + 1) * P], src[:, c * P:(c + 1) * P], ident)
                last.then_inc(*tick("pe", "pe", key))

            def heads(key, f, *deps, parts=1):
                out = product(pe, key, 512)
                for dep in deps:
                    pe.wait_ge(*done(*dep))
                for h in range(NT):
                    for j in range(parts):
                        l, r = f(h, j)
                        last = pe.matmul(out[:, h * P:(h + 1) * P], l, r, start=(j == 0), stop=(j == parts - 1))
                last.then_inc(*tick("pe", "pe", key))

            pe.wait_ge(*done("ones"))
            pe.wait_ge(*done("con_in"))
            for it in ITEMS:
                stage[0], k, l = it[0], it[0], it[1]
                if k == "ada":
                    g = it[2]
                    out = product(pe, it, 16)
                    pe.wait_ge(*done("csL"))
                    for i, u in enumerate(units_of(it)):
                        last = dense(u, out[:, 2 * i:2 * i + 2], csH, csL, [(0, 2)], KT)
                        last.then_inc(*tick("pe", "pe", u))
                elif k == "norm":
                    allsum(it, ones[:, :], lambda t, a, b: sqn[t % 2][:, a:b], TOK, lambda t: ("sqn", l, t), KT)
                elif k == "gb":
                    unit(units_of(it)[0], "gb")
                    out = product(pe, ("gturn", l), 1024)
                    pe.wait_ge(*done("cum", l, 0))
                    pe.wait_ge(*done("cum", l, 1))
                    pe.wait_ge(*done("beta", l))
                    for j in range(3):
                        src = (GR[0:16, :], GR[32:48, :], gbt[0][:, :])[j]
                        idn = ident[32:48, 32:48] if j == 1 else ident[0:16, 0:16]
                        for c in range(NC):
                            o = (0, 512, NC * 16)[j] + c * 16
                            last = pe.transpose(out[:, o:o + 16], src[:, c * P:(c + 1) * P], idn)
                    last.then_inc(*tick("pe", "pe", ("gturn", l)))
                elif k == "dqkv":
                    h, kind = it[2], it[3]
                    unit((kind, l, h), kind)
                    if kind == "dv":
                        turn(("vturn", l, h), vb[h % 2], TOK, ("silu", "dv", l, h))
                elif k == "dnorm":
                    h, kind = it[2], it[3]
                    n = ntok(l, kind)
                    allsum(it, ones[:, :], lambda t, a, b: sqd[0 if kind == "dk" else 1][:, a:b], n,
                           lambda t: ("sqd", kind, l, h), 1)
                    if kind == "dk":
                        turn(("kturn", l, h), kT[:, h, :], TOK, ("dn", "dk", l, h))
                elif k == "prep":
                    s = it[2]
                    live = l == 0 or s >= 2
                    for d in range(2):
                        ch = ORDER[d][s]
                        cc = slice(ch * P, (ch + 1) * P)
                        r0 = 32 * d
                        col = lambda h: r0 + 8 + 4 * d + h
                        heads(("G", l, s, d), lambda h, j: (ident[r0:r0 + 16, col(h):col(h) + 1].to_broadcast([16, P]),
                                                            GR[r0:r0 + 16, cc]), ("cum", l, d))
                        heads(("KK", l, s, d), lambda h, j: (kT[:, h, cc], kT[:, h, cc]), ("dn", "dk", l, 3))
                        if live:
                            heads(("QK", l, s, d), lambda h, j: (kT[:, h, cc], qT[:, h, cc]), ("dn", "dq", l, 3))
                    for lv in range(LEVELS):
                        if lv > 0:
                            for d in range(2):
                                b = db[d]
                                heads(("T1", l, s, d, lv), lambda h, j: (b["X"][:, h, :], b["EG"][:, h, :]),
                                      ("X", l, s, d, lv), ("M", l, s, d, lv - 1))
                            for d in range(2):
                                b = db[d]
                                heads(("PU", l, s, d, lv), lambda h, j: (b["E"][:, h, :], b["Pm"][:, h, :]),
                                      ("T1", l, s, d, lv), ("P", l, s, d, lv - 1))
                        if lv < LEVELS - 1:
                            for d in range(2):
                                out = product(pe, ("MT", l, s, d, lv), 512)
                                pe.wait_ge(*done("P", l, s, d, lv))
                                for h in range(NT):
                                    last = pe.transpose(out[:, h * P:(h + 1) * P], db[d]["Pm"][:, h, :], ident)
                                last.then_inc(*tick("pe", "pe", ("MT", l, s, d, lv)))
                elif k == "scan":
                    s = it[2]
                    live = l == 0 or s >= 2
                    for d in range(2):
                        b = db[d]
                        heads(("KS", l, s, d), lambda h, j: (b["Kg"][:, h, :], b["S"][:, h, :]),
                              ("Kg", l, s, d), ("S", l, s, d))
                    for d in range(2):
                        b = db[d]
                        heads(("Y", l, s, d), lambda h, j: (b["Pm"][:, h, :], b["vn"][:, h, :]),
                              ("R", l, s, d), ("P", l, s, d, LEVELS - 1))
                    for d in range(2):
                        b = db[d]
                        if live:
                            heads(("O", l, s, d), lambda h, j: ((b["S"][:, h, :], b["Qg"][:, h, :]) if j == 0 else
                                                                (b["vn"][:, h, :], b["intra"][:, h, :])),
                                  ("Qg", l, s, d), ("vn", l, s, d), ("intra", l, s, d), parts=2)
                    for d in range(2):
                        b = db[d]
                        ch = ORDER[d][s]
                        heads(("U", l, s, d), lambda h, j: (Ktm[:, ch, h, :], b["vs"][:, h, :]), ("vs", l, s, d))
                elif k == "dout":
                    h = it[2]
                    n = ntok(l, "dz")
                    allsum(it, ones[:, :], lambda t, a, b: do[h % 2][:, a:b], n, lambda t: ("dosq", l, h), 1)
                    unit(("dz", l, h), "dz")
                elif k == "glu":
                    unit(("val", l, it[2]), "val")
                    unit(("glu", l, it[2]), "glu")
                elif k == "mix":
                    n, p = it[2], it[3]
                    for u in units_of(it)[:2]:
                        unit(u, "gate")
                    u = ("branch%d" % n, l, p)
                    w = ntok(l, "gate")
                    for j in range(2):
                        out = product(pe, (u, j), w)
                        pe.wait_ge(*done("y", n, l, NT - 1))
                        last = dense(u, out, yH, yL, segs(w), NT, j * P, 2 * P)
                        last.then_inc(*tick("pe", "pe", (u, j)))
                    got[("pe", u)] = got[("pe", (u, 1))]
                elif k == "ln":
                    n = ntok(l, "cz")
                    allsum(("lnsum", l), ones[:, :], lambda t, a, b: acc[:, t, a + (HALO if a else 0):b + (HALO if a else 0)],
                           n, lambda t: ("conv", l, t), NT)
                    allsum(("lnvar", l), ones[:, :], lambda t, a, b: sqc[t % 2][:, a + (HALO if a else 0):b + (HALO if a else 0)],
                           n, lambda t: ("sqc", l, t), NT)
                elif k == "z":
                    unit(("cz", l, it[2]), "cz")
                elif k == "qkv":
                    h = it[2]
                    for j, kind in enumerate(("aq", "ak")):
                        unit((kind, l, h), kind)
                        dst = (qh, kh)[j][h % 2]
                        allsum(("ss", kind, l, h), blk, lambda t, a, b: at1[0][:, a:b], ntok(l, kind),
                               lambda t: ("asq", kind, l, h), 1)
                        out = product(pe, ("rot", kind, l, h), SEQ)
                        pe.wait_ge(*done("an", kind, l, h))
                        pe.matmul(out[:, 0:SEQ], rot, dst[:, 0:SEQ], start=True, stop=True).then_inc(*tick("pe", "pe", ("rot", kind, l, h)))
                    unit(("av", l, h), "av")
                    turn(("aturn", l, h), vr, TOK, ("vr", l, h))
                elif k == "att":
                    h = it[2]
                    nq = ntok(l, "aq") // P
                    q_, k_ = qh[h % 2], kh[h % 2]

                    def scores(qt):
                        keys = segs(TOK) if qt < 4 else [(SEQ, TOK)]
                        for m in range(2):
                            key = ("sc", l, h, qt, m)
                            out = product(pe, key, TOK)
                            pe.wait_ge(*done("rope", "aq", l, h))
                            pe.wait_ge(*done("rope", "ak", l, h))
                            r = slice(64 * m, 64 * m + 64)
                            o = 0
                            for a, b in keys:
                                last = pe.matmul(out[:, o:o + b - a], q_[r, qt * P:(qt + 1) * P], k_[r, a:b],
                                                 start=True, stop=True)
                                o += b - a
                            last.then_inc(*tick("pe", "pe", key))

                    scores(0)
                    for qt in range(nq):
                        n = NC if qt < 4 else CTX // P
                        if qt + 1 < nq:
                            scores(qt + 1)
                        turn(("pt", l, h, qt), Pa[qt % 2][0], n * P, ("mixp", l, h, qt))
                        key = ("o", l, h, qt)
                        out = product(pe, key, P)
                        pe.wait_ge(*done("aT", l, h, qt))
                        pe.wait_ge(*done("Va", l, h))
                        for c in range(n):
                            last = pe.matmul(out[:, 0:P], Va[h % 2][:, NC - n + c, :], aT[qt % 2][:, c, :],
                                             start=(c == 0), stop=(c == n - 1))
                        last.then_inc(*tick("pe", "pe", key))
                elif k == "aout":
                    h = it[2]
                    n = ntok(l, "az")
                    unit(("az", l, h), "az")
                    allsum(("oss", l, h), ones[:, :], lambda t, a, b: at1[0][:, a:b], n, lambda t: ("aosq", l, h), 1)
                elif k == "out":
                    w = ntok(l, "wout")
                    for u in units_of(it):
                        out = product(pe, u, w)
                        pe.wait_ge(*done("m", l, KT - 1))
                        last = dense(u, out, hH, hL, segs(w), KT)
                        last.then_inc(*tick("pe", "pe", u))

        @block.sync
        def _(sp):
            stage[0] = "start"
            sp.dma_start(cons[:, :], con).then_inc(*tick("small_in", "con_", by=16))
            sp.dma_start(vecs[:, :, :], vec).then_inc(*tick("small_in", "vec_", by=16))
            sp.dma_start(csb[:, :, :], cT).then_inc(*tick("small_in", "c_", by=16))
            sp.dma_start(lamt[:, :, :, :], lamr).then_inc(*tick("small_in", "con_in", by=16))

            sp.dma_start(xs[:, :, :], xT).then_inc(*tick("x_in", "x_in", 0, by=16))
            for w, u in enumerate(UNITS):
                i = w % 3
                if w >= 3:
                    sp.wait_ge(*done("lo", UNITS[w - 3]))
                sp.dma_start(raw[i][:, :], wstream[w]).then_inc(*tick("raw%d" % i, "raw", u, by=16))

        @block.scalar
        def _(act):
            stage[0] = "start"
            done_hi = [0]

            def ahead(u):
                while done_hi[0] < min(WIDX[u] + 3, len(UNITS)):
                    w = done_hi[0]
                    v = UNITS[w]
                    act.wait_ge(*done("raw", v))
                    if w >= 3:
                        act.wait_ge(*done("pe", UNITS[w - 3]))
                        act.wait_ge(*done("lo", UNITS[w - 3]))
                    act.activation(wH[w % 3][:, :], raw[w % 3][:, :], ACT.Copy).then_inc(*tick("act", "hi", v))
                    done_hi[0] += 1

            def rsqrt(src, dst, scale, e, key, readkey, n):
                act.wait_ge(*done("pe", readkey))
                ins = act.activation(dst[:, 0:n], place[readkey][:, 0:n], ACT.Ln, bias=e, scale=scale)
                ins.then_inc(*tick_read("act", readkey))
                act.wait_ge(*done("read", readkey, readers[readkey] - 1))
                act.activation(dst[:, 0:n], dst[:, 0:n], ACT.Exp, scale=-0.5).then_inc(*tick("act", *key))

            act.wait_ge(*done("con_in"))
            act.wait_ge(*done("misc"))
            act.activation(cs32[:, :, :], csb[:, :, :], ACT.Silu).then_inc(*tick("act", "cs32"))
            act.wait_ge(*done("cs32"))
            act.activation(csH[:, :, :], cs32[:, :, :], ACT.Copy).then_inc(*tick("act", "csH"))
            for l in range(DEPTH):
                act.activation(nega[:, l:l + 1], vecs[:, l, V_AL:V_AL + 1], ACT.Exp).then_inc(*tick("act", "aexp", l))
            act.wait_ge(*done("lamdot"))
            act.activation(lam_exp[:, :, :], lam_dot[:, :, :], ACT.Exp).then_inc(*tick("act", "lamexp"))

            for it in ITEMS:
                stage[0], k, l = it[0], it[0], it[1]
                if k == "ada":
                    for u in units_of(it):
                        ahead(u)
                elif k == "norm":
                    act.wait_ge(*(done("x_in", 0) if l == 0 else done("xnew", l - 1, KT - 1)))
                    for t in range(KT):
                        if t >= 2:
                            act.wait_ge(*done("pe", it, t - 2))
                        act.activation(sqn[t % 2][:, :], xs[:, t, :], ACT.Square).then_inc(*tick("act", "sqn", l, t))
                    rsqrt(None, rsn, 1.0 / D, eps, ("rsn", l), it, TOK)
                    for t in range(KT):
                        for p, (a, b) in enumerate(segs(TOK)):
                            act.wait_ge(*done("hn", l, t, p))
                            act.activation(hH[:, t, a:b], hn[t % 2][:, a:b], ACT.Identity,
                                             bias=ada[:, l, t, p:p + 1]).then_inc(*tick("act", "hH", l, t, p))
                elif k == "gb":
                    u = units_of(it)[0]
                    ahead(u)
                    act.wait_ge(*done("pe", u))
                    act.wait_ge(*done("h", l, KT - 1))
                    ps = place[u]
                    act.activation(gbt[0][:, :], ps[0:16, 0:TOK], ACT.Sigmoid).then_inc(*tick("act", "beta", l))
                    act.activation(gbt[1][:, :], ps[0:16, 0:TOK], ACT.Identity,
                                        bias=vecs[0:16, l, V_DT:V_DT + 1]).then_inc(*tick_read("act", u))
                    act.wait_ge(*done("read", u, 0))
                    act.activation(gbt[2][:, :], gbt[1][:, :], ACT.Abs).then_inc(*tick("act", "gabs", l))
                    act.wait_ge(*done("gabs", l))
                    act.activation(gbt[2][:, :], gbt[2][:, :], ACT.Exp, scale=-1.0).then_inc(*tick("act", "gexp", l))
                    act.wait_ge(*done("gexp", l))
                    act.activation(gbt[2][:, :], gbt[2][:, :], ACT.Ln, bias=1.0).then_inc(*tick("act", "gln", l))
                elif k == "dqkv":
                    h, kind = it[2], it[3]
                    u = (kind, l, h)
                    ahead(u)
                    n = ntok(l, kind)
                    i = (3 * h + ("dk", "dv", "dq").index(kind)) % 2
                    act.wait_ge(*done("pe", u))
                    act.wait_ge(*done("pad0", l))
                    if 3 * h + ("dk", "dv", "dq").index(kind) >= 2:
                        act.wait_ge(*done("c3", l, 3 * h + ("dk", "dv", "dq").index(kind) - 2))
                    j = 3 * h + ("dk", "dv", "dq").index(kind)
                    if n == TOK:
                        act.activation(pad3[i][:, SEQ + 2:TOK + 2], place[u][:, SEQ:TOK], ACT.Copy).then_inc(*tick("act", "p3c", l, j))
                    act.activation(pad3[i][:, 1:SEQ + 1], place[u][:, 0:SEQ], ACT.Copy).then_inc(*tick_read("act", u))
                    act.wait_ge(*done("c3", l, j))
                    if l:
                        act.wait_ge(*done("xw", l - 1, KT - 1))
                    if kind == "dv":
                        dst = vb[h % 2]
                        if h >= 2:
                            act.wait_ge(*done("pe", ("vturn", l, h - 2)))
                    else:
                        dst = (qT if kind == "dq" else kT)[:, h, :]
                    if n == TOK:
                        act.activation(dst[:, SEQ:TOK], c3[i][:, SEQ + 1:TOK + 1], ACT.Silu).then_inc(*tick("act", "silc", l, j))
                    act.activation(dst[:, 0:SEQ], c3[i][:, 0:SEQ], ACT.Silu).then_inc(*tick("act", "silu", kind, l, h))
                    if kind == "dv":
                        key = ("vturn", l, h)
                        act.wait_ge(*done("pe", key))
                        act.activation(Vtm[:, :, h, :], place[key][:, 0:TOK].rearrange("p (c e) -> p c e", c=NC),
                                            ACT.Copy).then_inc(*tick_read("act", key))
                elif k == "dnorm":
                    h, kind = it[2], it[3]
                    n = ntok(l, kind)
                    i = 0 if kind == "dk" else 1
                    if h:
                        act.wait_ge(*done("dn", kind, l, h - 1))
                    rsqrt(None, rsd[i], 1.0, eps, ("rsd", kind, l, h), it, n)
                    if kind == "dk":
                        key = ("kturn", l, h)
                        act.wait_ge(*done("pe", key))
                        act.activation(Ktm[:, :, h, :], place[key][:, 0:TOK].rearrange("p (c e) -> p c e", c=NC),
                                            ACT.Copy).then_inc(*tick_read("act", key))
                elif k == "prep":
                    s = it[2]
                    for d in range(2):
                        b = db[d]
                        g = ("G", l, s, d)
                        act.wait_ge(*done("pe", g))
                        if s:
                            act.wait_ge(*done("pe", ("T1", l, s - 1, d, LEVELS - 1)))
                        else:
                            act.wait_ge(*done("prepfree", l))
                        act.activation(b["EG"][:, :, :], v4(place[g]), ACT.Exp).then_inc(*tick_read("act", g))
                    for d in range(2):
                        b = db[d]
                        act.wait_ge(*done("E", l, s, d))
                        act.activation(b["E"][:, :, :], b["E"][:, :, :], ACT.Exp).then_inc(*tick("act", "DT", l, s, d))
                    for lv in range(LEVELS):
                        if lv > 0:
                            for d in range(2):
                                key = ("T1", l, s, d, lv)
                                act.wait_ge(*done("pe", key))
                                if lv == 1:
                                    act.wait_ge(*done("intra", l, s, d))
                                    act.wait_ge(*done("AT", l, s, d))
                                    act.wait_ge(*done("last", l, s, d))
                                else:
                                    act.wait_ge(*done("pe", ("PU", l, s, d, lv - 1)))
                                act.activation(db[d]["E"][:, :, :], v4(place[key]), ACT.Copy).then_inc(*tick_read("act", key))
                                got[key] = got[("read", key, 0)]
                        if lv < LEVELS - 1:
                            for d in range(2):
                                key = ("MT", l, s, d, lv)
                                act.wait_ge(*done("pe", key))
                                if lv == 0:
                                    act.wait_ge(*done("Kg", l, s, d))
                                    act.wait_ge(*done("Qg", l, s, d))
                                    act.wait_ge(*done("last", l, s, d))
                                act.activation(db[d]["EG"][:, :, :], v4(place[key]), ACT.Copy).then_inc(*tick_read("act", key))
                                got[("M", l, s, d, lv)] = got[("read", key, 0)]
                elif k == "dout":
                    h = it[2]
                    n = ntok(l, "dz")
                    rsqrt(None, do[2 + h % 2], 1.0 / P, eps, ("dors", l, h), it, n)
                    u = ("dz", l, h)
                    ahead(u)
                    act.wait_ge(*done("pe", u))
                    if h >= 2:
                        act.wait_ge(*done("y32", 1, l, h - 2))
                    act.activation(do[4 + h % 2][:, 0:n], place[u][:, 0:n], ACT.Silu).then_inc(*tick_read("act", u))
                    act.wait_ge(*done("y32", 1, l, h))
                    act.activation(yH[:, h, 0:n], do[6 + h % 2][:, 0:n], ACT.Copy).then_inc(*tick("act", "yh", 1, l, h))
                elif k == "glu":
                    t = it[2]
                    n = ntok(l, "glu")
                    if t == 0:
                        act.wait_ge(*done("padz", l))
                        act.dma_start(cs[:, :, :], rope).then_inc(*tick("rope_in", "rope_in", l, by=16))
                    ahead(("val", l, t))
                    ahead(("glu", l, t))
                    u = ("glu", l, t)
                    act.wait_ge(*done("pe", u))
                    act.wait_ge(*done("padz", l))
                    if t >= 2:
                        act.wait_ge(*done("glu", l, t - 2))
                    act.activation(gl[t % 2][:, 0:n], place[u][:, 0:n], ACT.Sigmoid).then_inc(*tick_read("act", u))
                elif k == "mix":
                    n_, p = it[2], it[3]
                    n = ntok(l, "gate")
                    for j, u in enumerate(units_of(it)[:2]):
                        ahead(u)
                        act.wait_ge(*done("pe", u))
                        prev = mixes[mixes.index(it) - 1] if mixes.index(it) else None
                        if prev:
                            act.wait_ge(*done("gm", prev, j))
                        if n_ == 1 and p == 0:
                            act.wait_ge(*done("glu", l, 3))
                            act.wait_ge(*done("y32", 1, l, 3))
                            act.wait_ge(*done("yl", 1, l, 3))
                        if n_ == 0 and p == 0:
                            act.wait_ge(*done("y32", 0, l, 3))
                        act.activation(sg[j][:, 0:n], place[u][:, 0:n], ACT.Sigmoid).then_inc(*tick_read("act", u))
                    ahead(units_of(it)[2])
                elif k == "ln":
                    n = ntok(l, "cz")
                    W = ACCW if n == TOK else SEQ
                    for t in range(NT):
                        act.wait_ge(*done("xc", l, t))
                        if t >= 2:
                            act.wait_ge(*done("pe", ("lnvar", l), t - 2))
                        act.activation(sqc[t % 2][:, 0:W], acc[:, t, 0:W], ACT.Square).then_inc(*tick("act", "sqc", l, t))
                    rsqrt(None, rsc, 1.0 / BW, lneps, ("rsc", l), ("lnvar", l), n)
                elif k == "z":
                    t = it[2]
                    n = ntok(l, "cz")
                    u = ("cz", l, t)
                    ahead(u)
                    act.wait_ge(*done("pe", u))
                    act.wait_ge(*done("rsc", l))
                    if t >= 2:
                        act.wait_ge(*done("y32", 0, l, t - 2))
                    act.activation(zt[t % 2][:, 0:n], place[u][:, 0:n], ACT.Silu).then_inc(*tick_read("act", u))
                    act.wait_ge(*done("xn", l, t))
                    for a, b in segs(n):
                        o = HALO if a else 0
                        act.activation(acc[:, t, a + o:b + o], acc[:, t, a + o:b + o], ACT.Silu,
                                         scale=vecs[:, l, V_LG + t:V_LG + t + 1],
                                         bias=vecs[:, l, V_LB + t:V_LB + t + 1]).then_inc(*tick("act", "lns", l, t, a))
                    act.wait_ge(*done("y32", 0, l, t))
                    act.activation(yH[:, t, 0:n], zt[2 + t % 2][:, 0:n], ACT.Copy).then_inc(*tick("act", "yh", 0, l, t))
                elif k == "qkv":
                    h = it[2]
                    for j, kind in enumerate(("aq", "ak")):
                        u = (kind, l, h)
                        n = ntok(l, kind)
                        ahead(u)
                        act.wait_ge(*done("pe", u))
                        if j == 0:
                            if h:
                                act.wait_ge(*done("pe", ("ss", "ak", l, h - 1)))
                            if h == 0:
                                act.wait_ge(*done("yl", 0, l, NT - 1))
                                act.wait_ge(*done("y32", 0, l, NT - 1))
                            elif h >= 2:
                                act.wait_ge(*done("pe", ("oss", l, h - 2)))
                        else:
                            act.wait_ge(*done("pe", ("ss", "aq", l, h)))
                        act.activation(at1[0][:, 0:n], place[u][:, 0:n], ACT.Square).then_inc(*tick("act", "asq", kind, l, h))
                        if j == 0:
                            if h:
                                act.wait_ge(*done("an", "ak", l, h - 1))
                            if h >= 2:
                                act.wait_ge(*done("ao", l, h - 2))
                        else:
                            act.wait_ge(*done("an", "aq", l, h))
                        rsqrt(None, at1[1], 1.0 / 64, eps, ("ars", kind, l, h), ("ss", kind, l, h), n)
                    u = ("av", l, h)
                    ahead(u)
                    act.wait_ge(*done("pe", u))
                    if h:
                        act.wait_ge(*done("pe", ("aturn", l, h - 1)))
                    if h >= 2:
                        act.wait_ge(*done("y32", 2, l, h - 2))
                        act.wait_ge(*done("yl", 2, l, h - 2))
                        act.wait_ge(*done("yh", 2, l, h - 2))
                    act.activation(vr[:, :], place[u][:, 0:TOK], ACT.Copy).then_inc(*tick_read("act", u))
                    got[("vr", l, h)] = got[("read", u, 0)]
                    key = ("aturn", l, h)
                    act.wait_ge(*done("pe", key))
                    if h >= 2:
                        act.wait_ge(*done("pe", ("o", l, h - 2, ntok(l, "aq") // P - 1)))
                    act.activation(Va[h % 2][:, :, :].rearrange("p c e -> p (c e)"), place[key][:, 0:TOK], ACT.Copy).then_inc(*tick_read("act", key))
                    got[("Va", l, h)] = got[("read", key, 0)]
                elif k == "att":
                    h = it[2]
                    nq = ntok(l, "aq") // P

                    def soft(qt):
                        w = TOK if qt < 4 else CTX
                        i = qt % 2
                        for m in range(2):
                            key = ("sc", l, h, qt, m)
                            act.wait_ge(*done("pe", key))
                            act.wait_ge(*done("nmx", l, h, qt))
                            if qt >= 2:
                                act.wait_ge(*done("pe", ("pt", l, h, qt - 2)))
                            elif h:
                                act.wait_ge(*done("pe", ("pt", l, h - 1, nq - 2 + i)))
                            act.activation(Pa[i][m][:, 0:w], place[key][:, 0:w], ACT.Exp,
                                                bias=stat[:, i, 2 + m:3 + m], accum_out=stat[:, i, 4 + m:5 + m]).then_inc(*tick_read("act", key))

                    soft(0)
                    for qt in range(nq):
                        if qt + 1 < nq:
                            soft(qt + 1)
                        w = TOK if qt < 4 else CTX
                        key = ("pt", l, h, qt)
                        act.wait_ge(*done("pe", key))
                        if qt >= 2:
                            act.wait_ge(*done("pe", ("o", l, h, qt - 2)))
                        elif h:
                            act.wait_ge(*done("pe", ("o", l, h - 1, nq - 2 + qt % 2)))
                        act.activation(aT[qt % 2][:, :, :].rearrange("p c e -> p (c e)")[:, 0:w],
                                            place[key][:, 0:w], ACT.Copy).then_inc(*tick_read("act", key))
                        got[("aT", l, h, qt)] = got[("read", key, 0)]
                elif k == "aout":
                    h = it[2]
                    n = ntok(l, "az")
                    u = ("az", l, h)
                    ahead(u)
                    act.wait_ge(*done("ocopy", l, h, n // P - 1))
                    act.wait_ge(*done("pe", ("ss", "ak", l, min(h + 1, 3))))
                    if h:
                        act.wait_ge(*done("pe", ("oss", l, h - 1)))
                        act.wait_ge(*done("ao", l, h - 1))
                        act.wait_ge(*done("yl", 2, l, h - 1))
                    act.activation(at1[0][:, 0:n], at1[2][:, 0:n], ACT.Square).then_inc(*tick("act", "aosq", l, h))
                    act.wait_ge(*done("an", "ak", l, min(h + 1, 3)))
                    act.wait_ge(*done("pe", ("aturn", l, min(h + 1, 3))))
                    rsqrt(None, at1[1], 1.0 / P, eps, ("aors", l, h), ("oss", l, h), n)
                    act.wait_ge(*done("pe", u))
                    act.activation(vr[:, 0:n], place[u][:, 0:n], ACT.Silu).then_inc(*tick_read("act", u))
                    act.wait_ge(*done("y32", 2, l, h))
                    act.activation(yH[:, h, 0:n], vr[:, 0:n], ACT.Copy).then_inc(*tick("act", "yh", 2, l, h))
                elif k == "out":
                    n = ntok(l, "wout")
                    act.wait_ge(*done("pe", ("branch2", l, 3)))
                    act.dma_start(xs[:, :, 0:n], xT[:, :, 0:n] if l == 0 else xscr[:, :, 0:n]).then_inc(*tick("x_in", "x_back", l, by=16))
                    for t in range(KT):
                        act.wait_ge(*done("gadd", l, 2, t))
                        act.activation(hH[:, t, 0:n], mT[:, t, 0:n], ACT.Copy).then_inc(*tick("act", "mH", l, t))
                    for d, u in enumerate(units_of(it)):
                        ahead(u)
                        act.wait_ge(*done("xnew", l, d))
                        dst = xscr[:, d, :] if l < DEPTH - 1 else outT[:, d, :]
                        act.dma_start(dst, xs[:, d, 0:n]).then_inc(*tick("x_out", "xw", l, d, by=16))
            act.wait_ge(*done("xw", DEPTH - 1, KT - 1))

        @block.vector
        def _(dve):
            stage[0] = "start"
            def col(l, c, rows=P):
                return vecs[0:rows, l, c:c + 1]

            dve.wait_ge(*done("con_in"))
            dve.wait_ge(*done("misc"))
            for l in range(DEPTH):
                for j in range(2):
                    dve.tensor_tensor(lamp[:, l, j, :], lamt[:, l, 2 * j, :], lamt[:, l, 2 * j + 1, :], ALU.mult).then_inc(*tick("dve", "lamp", l, j))
            dve.wait_ge(*done("lamp", 1, 1))
            dve.tensor_reduce(lam_dot[:, :, :], lamp[:, :, :, :], AX_X, ALU.add).then_inc(*tick("dve", "lamdot"))
            dve.wait_ge(*done("cs32"))
            dve.wait_ge(*done("csH"))
            dve.tensor_tensor(csL[:, :, :], cs32[:, :, :], csH[:, :, :].bitcast(F32), ALU.subtract).then_inc(*tick("dve", "csL_"))
            got[("csL",)] = got[("csL_",)]
            for l in range(DEPTH):
                lam0 = 0.8 - 0.6 * math.exp(-0.3 * l)
                dve.tensor_scalar(qg8[:, l:l + 1], col(l, V_QG), 64 ** -0.5, None, ALU.mult).then_inc(*tick("dve", "qg8", l))
                dve.tensor_scalar(sub1[:, l:l + 1], col(l, V_SUB), 1.0 - lam0, None, ALU.mult).then_inc(*tick("dve", "sub1", l))
                dve.wait_ge(*done("aexp", l))
                dve.tensor_scalar(nega[:, l:l + 1], nega[:, l:l + 1], -1.0, None, ALU.mult).then_inc(*tick("dve", "nega", l))
                dve.wait_ge(*done("lamexp"))
                dve.tensor_tensor(nlam[:, l:l + 1], lam_exp[:, l, 1:2], lam_exp[:, l, 0:1], ALU.subtract).then_inc(*tick("dve", "nl0", l))
                dve.wait_ge(*done("nl0", l))
                dve.tensor_scalar(nlam[:, l:l + 1], nlam[:, l:l + 1], -lam0, None, ALU.add).then_inc(*tick("dve", "nlam", l))

            conv_steps = []
            conv_done = [0]

            def conv(l, n):
                W = ACCW if ntok(l, "val") == TOK else SEQ
                for _ in range(n):
                    if conv_done[0] >= 2 * CK:
                        return
                    pr, k = divmod(conv_done[0], CK)
                    conv_done[0] += 1
                    for t in (2 * pr, 2 * pr + 1):
                        w = col(l, V_CW + t * CK + k)
                        if k == 0:
                            dve.wait_ge(*done("glu", l, t))
                            ins = dve.tensor_scalar(acc[:, t, 0:W], padc[:, t, 0:W], w, col(l, V_CB + t),
                                                    ALU.mult, ALU.add)
                        else:
                            dve.wait_ge(*done("tap", l, t, k - 1))
                            ins = dve.scalar_tensor_tensor(acc[:, t, 0:W], padc[:, t, k:k + W], w, acc[:, t, 0:W],
                                                           ALU.mult, ALU.add)
                        ins.then_inc(*tick("dve", "tap", l, t, k))
                        if k == CK - 1:
                            got[("conv", l, t)] = got[("tap", l, t, k)]

            for it in ITEMS:
                stage[0], k, l = it[0], it[0], it[1]
                if k == "ada":
                    g = it[2]
                    dve.wait_ge(*done("pe", units_of(it)[7]))
                    dve.tensor_tensor(ada[:, l, 8 * g:8 * g + 8, :], place[it][:, 0:16].rearrange("p (m c) -> p m c", c=2),
                                           bc(vecs[:, l, V_BADA + 8 * g:V_BADA + 8 * g + 8], 2), ALU.add).then_inc(*tick_read("dve", it))
                    got[it] = got[("read", it, 0)]
                    if g == 1:
                        dve.wait_ge(*done(*it))
                        dve.scalar_tensor_tensor(gs[:, l, :, :], ada[:, l, 8:16, :], 1.0,
                                                   bc(vecs[:, l, V_NG:V_NG + KT], 2), ALU.add, ALU.mult).then_inc(*tick("dve", "gs", l))
                elif k == "norm":
                    dve.wait_ge(*done("gs", l))
                    dve.wait_ge(*done("rsn", l))
                    dve.wait_ge(*done("ada", l, 0))
                    if l:
                        dve.wait_ge(*done("pe", ("wout", l - 1, KT - 1)))
                    for t in range(KT):
                        for p, (a, b) in enumerate(segs(TOK)):
                            if t >= 2:
                                dve.wait_ge(*done("h", l, t - 2))
                                dve.wait_ge(*done("hH", l, t - 2, p))
                            dve.scalar_tensor_tensor(hn[t % 2][:, a:b], xs[:, t, a:b], gs[:, l, t, p:p + 1],
                                                       rsn[:, a:b], ALU.mult, ALU.mult).then_inc(*tick("dve", "hn", l, t, p))
                        if t:
                            lowh(l, t - 1)
                    lowh(l, KT - 1)
                elif k == "gb":
                    dve.wait_ge(*done("gln", l))
                    dve.wait_ge(*done("rm", l))
                    dve.wait_ge(*done("nega", l))
                    dve.scalar_tensor_tensor(gbt[1][:, :], gbt[1][:, :], 0.0, gbt[2][:, :], ALU.max, ALU.add).then_inc(*tick("dve", "sp", l))
                    dve.wait_ge(*done("sp", l))
                    dve.tensor_scalar(gbt[1][:, :], gbt[1][:, :], nega[0:16, l:l + 1], None, ALU.mult).then_inc(*tick("dve", "g", l))
                    dve.wait_ge(*done("g", l))
                    dve.tensor_tensor_scan(GR[0:16, :], gbt[3][:, :], gbt[1][:, :], 0.0, ALU.mult, ALU.add).then_inc(*tick("dve", "cum", l, 0))
                    dve.tensor_tensor_scan(GR[32:48, ::-1], gbt[3][:, :], gbt[1][:, ::-1], 0.0, ALU.mult, ALU.add).then_inc(*tick("dve", "cum", l, 1))
                    key = ("gturn", l)
                    dve.wait_ge(*done("pe", key))
                    for d in range(2):
                        dve.tensor_copy(gcol[:, d, :, :].rearrange("p c x -> p (c x)"),
                                          place[key][:, 512 * d:512 * d + NC * 16]).then_inc(*tick("dve", "gcol", l))
                    dve.tensor_copy(bcol[:, :, :].rearrange("p c x -> p (c x)"), place[key][:, NC * 16:2 * NC * 16]).then_inc(*tick_read("dve", key))
                    got[("bcol", l)] = got[("read", key, 0)]
                elif k == "dqkv":
                    h, kind = it[2], it[3]
                    j = 3 * h + ("dk", "dv", "dq").index(kind)
                    i = j % 2
                    n = ntok(l, kind)
                    W = TOK + 1 if n == TOK else SEQ
                    w0 = V_DW + 3 * (NT * ("dq", "dk", "dv").index(kind) + h)
                    dve.wait_ge(*done("read", (kind, l, h), 0))
                    if n == TOK:
                        dve.wait_ge(*done("p3c", l, j))
                    if j >= 2:
                        ok, oh = ("dk", "dv", "dq")[(j - 2) % 3], (j - 2) // 3
                        dve.wait_ge(*done("silu", ok, l, oh))
                    dve.tensor_scalar(c3[i][:, 0:W], pad3[i][:, 0:W], col(l, w0), None, ALU.mult).then_inc(*tick("dve", "c3a", l, j))
                    dve.wait_ge(*done("c3a", l, j))
                    dve.scalar_tensor_tensor(c3[i][:, 0:W], pad3[i][:, 1:1 + W], col(l, w0 + 1), c3[i][:, 0:W],
                                               ALU.mult, ALU.add).then_inc(*tick("dve", "c3b", l, j))
                    dve.wait_ge(*done("c3b", l, j))
                    dve.scalar_tensor_tensor(c3[i][:, 0:W], pad3[i][:, 2:2 + W], col(l, w0 + 2), c3[i][:, 0:W],
                                               ALU.mult, ALU.add).then_inc(*tick("dve", "c3", l, j))
                elif k == "dnorm":
                    h, kind = it[2], it[3]
                    n = ntok(l, kind)
                    dst = (qT if kind == "dq" else kT)[:, h, 0:n]
                    i = 0 if kind == "dk" else 1
                    dve.wait_ge(*done("rsd", kind, l, h))
                    dve.wait_ge(*done("silu", kind, l, h))
                    dve.scalar_tensor_tensor(dst, dst, P ** -0.5 if kind == "dq" else 1.0, rsd[i][:, 0:n],
                                               ALU.mult, ALU.mult).then_inc(*tick("dve", "dn", kind, l, h))
                elif k == "prep":
                    s = it[2]
                    live = l == 0 or s >= 2
                    for d in range(2):
                        b = db[d]
                        g = ("G", l, s, d)
                        dve.wait_ge(*done("read", g, 0))
                        dve.wait_ge(*done("gcol", l))
                        if s:
                            dve.wait_ge(*done("pe", ("PU", l, s - 1, d, LEVELS - 1)))
                        else:
                            dve.wait_ge(*done("prepfree", l))
                        for h in range(NT):
                            c = 8 + 4 * d + h
                            ins = dve.scalar_tensor_tensor(b["E"][:, h, :], place[g][:, h * P:(h + 1) * P],
                                                           gcol[:, d, ORDER[d][s], c:c + 1], neg(d), ALU.subtract, ALU.add)
                        ins.then_inc(*tick_read("dve", g))
                        got[("E", l, s, d)] = got[("read", g, readers[g] - 1)]
                    for d in range(2):
                        b = db[d]
                        key = ("KK", l, s, d)
                        dve.wait_ge(*done("pe", key))
                        dve.wait_ge(*done("DT", l, s, d))
                        if s:
                            dve.wait_ge(*done("X", l, s - 1, d, LEVELS - 1))
                        dve.tensor_tensor(b["AT"][:, :, :], v4(place[key]), b["E"][:, :, :], ALU.mult).then_inc(*tick_read("dve", key))
                        got[("AT", l, s, d)] = got[("read", key, 0)]
                        if live:
                            key = ("QK", l, s, d)
                            dve.wait_ge(*done("pe", key))
                            if s and (l == 0 or s - 1 >= 2):
                                dve.wait_ge(*done("pe", ("O", l, s - 1, d)))
                            dve.tensor_tensor(b["intra"][:, :, :], v4(place[key]), b["E"][:, :, :], ALU.mult).then_inc(*tick_read("dve", key))
                            got[("intra", l, s, d)] = got[("read", key, 0)]
                        else:
                            got[("intra", l, s, d)] = got[("AT", l, s, d)]
                    for lv in range(1, LEVELS):
                        for d in range(2):
                            b = db[d]
                            key = ("PU", l, s, d, lv)
                            dve.wait_ge(*done("pe", key))
                            dve.wait_ge(*done("P", l, s, d, lv - 1))
                            if lv == 1:
                                dve.wait_ge(*done("P", l, s, d, 0))
                            dve.wait_ge(*done("pe", ("MT", l, s, d, lv - 1)))
                            dve.tensor_tensor(b["Pm"][:, :, :], b["Pm"][:, :, :], v4(place[key]), ALU.subtract).then_inc(*tick_read("dve", key))
                            got[("P", l, s, d, lv)] = got[("read", key, 0)]
                elif k == "scan":
                    s = it[2]
                    live = l == 0 or s >= 2
                    for d in range(2):
                        b = db[d]
                        ch = ORDER[d][s]
                        key = ("KS", l, s, d)
                        dve.wait_ge(*done("pe", key))
                        dve.wait_ge(*done("read", ("vturn", l, 3), 0))
                        if s:
                            dve.wait_ge(*done("vs", l, s - 1, d))
                            if l == 0 or s - 1 >= 2:
                                dve.wait_ge(*done("pe", ("O", l, s - 1, d)))
                        dve.tensor_tensor(b["vn"][:, :, :], Vtm[:, ch, :, :], v4(place[key]), ALU.subtract).then_inc(*tick_read("dve", key))
                        got[("R", l, s, d)] = got[("read", key, 0)]
                    for d in range(2):
                        b = db[d]
                        key = ("Y", l, s, d)
                        dve.wait_ge(*done("pe", key))
                        dve.wait_ge(*done("bcol", l))
                        dve.tensor_tensor(b["vn"][:, :, :], v4(place[key]),
                                               bc(bcol[:, ORDER[d][s], 4 * d:4 * d + 4]), ALU.mult).then_inc(*tick_read("dve", key))
                        got[("vn", l, s, d)] = got[("read", key, 0)]
                    for d in range(2):
                        ch = ORDER[d][s]
                        if live:
                            key = ("O", l, s, d)
                            dst = oT[:, :, ch * P:(ch + 1) * P]
                            other = ORDER[1 - d].index(ch)
                            dve.wait_ge(*done("pe", key))
                            if (other, 1 - d) < (s, d):
                                dve.wait_ge(*done("oT", l, other, 1 - d))
                                ins = dve.tensor_tensor(dst, dst, v4(place[key]), ALU.add)
                            else:
                                ins = dve.tensor_copy(dst, v4(place[key]))
                            ins.then_inc(*tick_read("dve", key))
                            got[("oT", l, s, d)] = got[("read", key, 0)]
                    for d in range(2):
                        b = db[d]
                        key = ("U", l, s, d)
                        dve.wait_ge(*done("pe", key))
                        dve.wait_ge(*done("Se", l, s, d))
                        dve.tensor_tensor(b["S"][:, :, :], b["S"][:, :, :], v4(place[key]), ALU.add).then_inc(*tick_read("dve", key))
                        got[("S", l, s + 1, d)] = got[("read", key, 0)]
                elif k == "dout":
                    h = it[2]
                    n = ntok(l, "dz")
                    dve.wait_ge(*done("dors", l, h))
                    dve.scalar_tensor_tensor(do[8 + h % 2][:, 0:n], oT[:, h, 0:n], col(l, V_DNG), do[2 + h % 2][:, 0:n],
                                               ALU.mult, ALU.mult).then_inc(*tick("dve", "don", l, h))
                    dve.wait_ge(*done("don", l, h))
                    dve.wait_ge(*done("read", ("dz", l, h), 0))
                    if h >= 2:
                        dve.wait_ge(*done("yh", 1, l, h - 2))
                        dve.wait_ge(*done("yl", 1, l, h - 2))
                    dve.tensor_tensor(do[6 + h % 2][:, 0:n], do[8 + h % 2][:, 0:n], do[4 + h % 2][:, 0:n], ALU.mult).then_inc(*tick("dve", "y32", 1, l, h))
                elif k == "glu":
                    t = it[2]
                    n = ntok(l, "glu")
                    dve.wait_ge(*done("read", ("glu", l, t), 0))
                    dve.wait_ge(*done("pe", ("val", l, t)))
                    dve.wait_ge(*done("padz", l))
                    ps = place[("val", l, t)]
                    if n == TOK:
                        o = 2 * HALO + SEQ
                        dve.tensor_tensor(padc[:, t, o:o + CTX], ps[:, SEQ:TOK], gl[t % 2][:, SEQ:TOK], ALU.mult).then_inc(*tick("dve", "gluc", l, t))
                    dve.tensor_tensor(padc[:, t, HALO:HALO + SEQ], ps[:, 0:SEQ], gl[t % 2][:, 0:SEQ], ALU.mult).then_inc(*tick_read("dve", ("val", l, t)))
                    got[("glu", l, t)] = got[("read", ("val", l, t), 0)]
                    if t == 0:
                        conv_done[0] = 0
                    elif t < 3:
                        conv(l, 8)
                elif k == "mix":
                    n_, p = it[2], it[3]
                    n = ntok(l, "gate")
                    for j in range(2):
                        d = 2 * p + j
                        if n_ == 1:
                            conv(l, 7)
                        u = ("branch%d" % n_, l, p)
                        gu = ("gate%d" % n_, l, d)
                        dve.wait_ge(*done("pe", (u, j)))
                        dve.wait_ge(*done("read", gu, 0))
                        if n_ == 1:
                            dst = mT[:, d, 0:n]
                        else:
                            dst = gm[:, 0:n]
                            i = mixes.index(it)
                            dve.wait_ge(*(done("gadd", l, n_, d - 1) if d else done("gadd", l, {0: 1, 2: 0}[n_], KT - 1)))
                        dve.tensor_tensor(dst, place[(u, j)][:, 0:n], sg[j][:, 0:n], ALU.mult).then_inc(*tick_read("dve", (u, j)))
                        got[("gm", it, j)] = got[("read", (u, j), 0)]
                        if n_ == 1:
                            got[("gadd", l, 1, d)] = got[("gm", it, j)]
                    if n_ == 1 and p == 3:
                        conv(l, 2 * CK)
                elif k == "ln":
                    n = ntok(l, "cz")
                    key = ("lnsum", l)
                    dve.wait_ge(*done("pe", key))
                    for t in range(NT):
                        dve.wait_ge(*done("tap", l, t, CK - 1))
                        if n == TOK:
                            dve.scalar_tensor_tensor(acc[:, t, SEQ + HALO:ACCW], place[key][:, SEQ:TOK], -1.0 / BW,
                                                       acc[:, t, SEQ + HALO:ACCW], ALU.mult, ALU.add).then_inc(*tick("dve", "xcc", l, t))
                        ins = dve.scalar_tensor_tensor(acc[:, t, 0:SEQ], place[key][:, 0:SEQ], -1.0 / BW,
                                                       acc[:, t, 0:SEQ], ALU.mult, ALU.add)
                        if t == NT - 1:
                            ins.then_inc(*tick_read("dve", key))
                            got[("xc", l, t)] = got[("read", key, 0)]
                        else:
                            ins.then_inc(*tick("dve", "xc", l, t))
                elif k == "z":
                    t = it[2]
                    n = ntok(l, "cz")
                    dve.wait_ge(*done("read", ("cz", l, t), 0))
                    dve.wait_ge(*done("lns", l, t, 0))
                    if t >= 2:
                        dve.wait_ge(*done("yh", 0, l, t - 2))
                        dve.wait_ge(*done("yl", 0, l, t - 2))
                    if n == TOK:
                        dve.wait_ge(*done("lns", l, t, SEQ))
                        dve.tensor_tensor(zt[2 + t % 2][:, SEQ:TOK], acc[:, t, SEQ + HALO:ACCW], zt[t % 2][:, SEQ:TOK],
                                            ALU.mult).then_inc(*tick("dve", "y32c", 0, l, t))
                    dve.tensor_tensor(zt[2 + t % 2][:, 0:SEQ], acc[:, t, 0:SEQ], zt[t % 2][:, 0:SEQ], ALU.mult).then_inc(*tick("dve", "y32", 0, l, t))
                elif k == "qkv":
                    h = it[2]
                    for j, kind in enumerate(("aq", "ak")):
                        u = (kind, l, h)
                        n = ntok(l, kind)
                        dst = (qh, kh)[j][h % 2]
                        g = qg8[:, l:l + 1] if j == 0 else col(l, V_KG)
                        dve.wait_ge(*done("ars", kind, l, h))
                        dve.wait_ge(*done("qg8", l))
                        if h >= 2:
                            dve.wait_ge(*done("pe", ("sc", l, h - 2, ntok(l, "aq") // P - 1, 1)))
                        dve.scalar_tensor_tensor(dst[:, 0:n], place[u][:, 0:n], g, at1[1][:, 0:n],
                                                      ALU.mult, ALU.mult).then_inc(*tick_read("dve", u))
                        got[("an", kind, l, h)] = got[("read", u, 0)]
                        key = ("rot", kind, l, h)
                        dve.wait_ge(*done("pe", key))
                        dve.wait_ge(*done("rope_in", l))
                        if j:
                            dve.wait_ge(*done("rope", "aq", l, h))
                        elif h:
                            dve.wait_ge(*done("rope", "ak", l, h - 1))
                        dve.tensor_tensor(at1[2][:, 0:SEQ], place[key][:, 0:SEQ], cs[:, 1, :], ALU.mult).then_inc(*tick_read("dve", key))
                elif k == "att":
                    h = it[2]
                    nq = ntok(l, "aq") // P

                    def maxes(qt):
                        w = TOK if qt < 4 else CTX
                        i = qt % 2
                        for m in range(2):
                            key = ("sc", l, h, qt, m)
                            dve.wait_ge(*done("pe", key))
                            dve.tensor_reduce(stat[:, i, m:m + 1], place[key][:, 0:w], AX_X, ALU.max).then_inc(*tick("dve", "mx", l, h, qt, m))
                        dve.wait_ge(*done("mx", l, h, qt, 1))
                        dve.tensor_scalar(stat[:, i, 2:4], stat[:, i, 0:2], -1.0, None, ALU.mult).then_inc(*tick("dve", "nmx", l, h, qt))

                    maxes(0)
                    for qt in range(nq):
                        w = TOK if qt < 4 else CTX
                        i = qt % 2
                        if qt + 1 < nq:
                            maxes(qt + 1)
                        dve.wait_ge(*done("read", ("sc", l, h, qt, 1), 0))
                        dve.wait_ge(*done("nlam", l))
                        dve.reciprocal(stat[:, i, 6:8], stat[:, i, 4:6]).then_inc(*tick("dve", "rc", l, h, qt))
                        dve.wait_ge(*done("rc", l, h, qt))
                        dve.tensor_scalar(c1[:, i:i + 1], stat[:, i, 7:8], nlam[:, l:l + 1], None, ALU.mult).then_inc(*tick("dve", "c1", l, h, qt))
                        dve.wait_ge(*done("c1", l, h, qt))
                        dve.tensor_scalar(Pa[i][1][:, 0:w], Pa[i][1][:, 0:w], c1[:, i:i + 1], None, ALU.mult).then_inc(*tick("dve", "p1", l, h, qt))
                        dve.wait_ge(*done("p1", l, h, qt))
                        dve.scalar_tensor_tensor(Pa[i][0][:, 0:w], Pa[i][0][:, 0:w], stat[:, i, 6:7], Pa[i][1][:, 0:w],
                                                   ALU.mult, ALU.add).then_inc(*tick("dve", "mixp", l, h, qt))
                        if qt:
                            ocopy(l, h, qt - 1)
                    ocopy(l, h, nq - 1)
                elif k == "aout":
                    h = it[2]
                    n = ntok(l, "az")
                    dve.wait_ge(*done("aors", l, h))
                    dve.wait_ge(*done("ocopy", l, h, n // P - 1))
                    dve.scalar_tensor_tensor(at1[2][:, 0:n], at1[2][:, 0:n], sub1[:, l:l + 1], at1[1][:, 0:n],
                                               ALU.mult, ALU.mult).then_inc(*tick("dve", "aon", l, h))
                    dve.wait_ge(*done("aon", l, h))
                    dve.wait_ge(*done("read", ("az", l, h), 0))
                    dve.tensor_tensor(vr[:, 0:n], at1[2][:, 0:n], vr[:, 0:n], ALU.mult).then_inc(*tick("dve", "y32", 2, l, h))
                    got[("ao", l, h)] = got[("y32", 2, l, h)]
                elif k == "out":
                    n = ntok(l, "wout")
                    for t in range(KT):
                        dve.wait_ge(*done("mH", l, t))
                        dve.wait_ge(*done("gadd", l, 2, t))
                        dve.tensor_tensor(hL[:, t, 0:n], mT[:, t, 0:n], hH[:, t, 0:n].bitcast(F32), ALU.subtract).then_inc(*tick("dve", "m", l, t))
                    for t, u in enumerate(units_of(it)):
                        dve.wait_ge(*done("pe", u))
                        dve.wait_ge(*done("x_back", l))
                        for p, (a, b) in list(enumerate(segs(n)))[::-1]:
                            ins = dve.scalar_tensor_tensor(xs[:, t, a:b], place[u][:, a:b], ada[:, l, 16 + t, p:p + 1],
                                                           xs[:, t, a:b], ALU.mult, ALU.add)
                            if p == 0:
                                ins.then_inc(*tick_read("dve", u))
                            else:
                                ins.then_inc(*tick("dve", "xnc", l, t))
                        got[("xnew", l, t)] = got[("read", u, 0)]

        @block.gpsimd
        def _(pool):
            stage[0] = "start"
            done_lo = [0]

            def ahead(u):
                while done_lo[0] < min(WIDX[u] + 3, len(UNITS)):
                    w = done_lo[0]
                    v = UNITS[w]
                    pool.wait_ge(*done("hi", v))
                    pool.tensor_tensor(wL[w % 3][:, :], raw[w % 3][:, :], wH[w % 3][:, :].bitcast(F32), ALU.subtract).then_inc(*tick("pool", "lo", v))
                    done_lo[0] += 1

            def lowy(n_, l, h, n, y32):
                pool.wait_ge(*done("yh", n_, l, h))
                pool.tensor_tensor(yL[:, h, 0:n], y32[:, 0:n], yH[:, h, 0:n].bitcast(F32), ALU.subtract).then_inc(*tick("pool", "yl", n_, l, h))
                got[("y", n_, l, h)] = got[("yl", n_, l, h)]

            pool.memset(ones[:, :], 1.0).then_inc(*tick("pool", "ones_"))
            pool.memset(misc[:, 0:1], RMS_EPS).then_inc(*tick("pool", "misc0"))
            pool.memset(misc[:, 1:2], LN_EPS).then_inc(*tick("pool", "misc_"))
            got[("ones",)] = got[("misc",)] = got[("misc_",)]

            for it in ITEMS:
                stage[0], k, l = it[0], it[0], it[1]
                if k == "ada":
                    for u in units_of(it):
                        ahead(u)
                elif k == "gb":
                    pool.wait_ge(*done("h", l, KT - 1))
                    pool.memset(gbt[3][:, :], 1.0).then_inc(*tick("pool", "rm1", l))
                    pool.wait_ge(*done("rm1", l))
                    pool.memset(gbt[3][:, ::P], 0.0).then_inc(*tick("pool", "rm", l))
                    for i in range(2):
                        for c in (0, SEQ + 1, TOK + 2):
                            pool.memset(pad3[i][:, c:c + 1], 0.0).then_inc(*tick("pool", "pad0", l))
                    ahead(units_of(it)[0])
                elif k == "dqkv":
                    ahead(units_of(it)[0])
                elif k == "dnorm":
                    h, kind = it[2], it[3]
                    n = ntok(l, kind)
                    i = 0 if kind == "dk" else 1
                    src = (qT if kind == "dq" else kT)[:, h, 0:n]
                    pool.wait_ge(*done("silu", kind, l, h))
                    if h:
                        pool.wait_ge(*done("pe", ("dnorm", l, h - 1, kind)))
                    pool.tensor_tensor(sqd[i][:, 0:n], src, src, ALU.mult).then_inc(*tick("pool", "sqd", kind, l, h))
                elif k == "prep":
                    s = it[2]
                    live = l == 0 or s >= 2
                    if s == 0:
                        pool.wait_ge(*done("dn", "dq", l, 3))
                        pool.wait_ge(*done("dn", "dk", l, 3))
                        pool.wait_ge(*done("read", ("kturn", l, 3), 0))
                        pool.wait_ge(*done("read", ("vturn", l, 3), 0))
                        pool.wait_ge(*done("bcol", l))
                        for d in range(2):
                            pool.memset(db[d]["S"][:, :, :], 0.0).then_inc(*tick("pool", "S", l, 0, d))
                        got[("prepfree", l)] = got[("S", l, 0, 1)]
                    for d in range(2):
                        b = db[d]
                        ch = ORDER[d][s]
                        cc = slice(ch * P, (ch + 1) * P)
                        lc = P - 1 if d == 0 else 0
                        pool.wait_ge(*done("read", ("G", l, s, d), 0))
                        pool.wait_ge(*done("DT", l, s, d))
                        pool.tensor_copy(lastc[:, d, 0, :], b["E"][:, :, lc]).then_inc(*tick("pool", "last0", l, s, d))
                        pool.tensor_copy(lastc[:, d, 1, :], b["EG"][:, :, lc]).then_inc(*tick("pool", "last", l, s, d))
                        pool.wait_ge(*done("AT", l, s, d))
                        pool.tensor_tensor(b["AT"][:, :, :], b["AT"][:, :, :], bc(bcol[:, ch, 4 * d:4 * d + 4]),
                                             ALU.mult).then_inc(*tick("pool", "ATb", l, s, d))
                        pool.wait_ge(*done("ATb", l, s, d))
                        pool.tensor_tensor(b["X"][:, :, :], b["AT"][:, :, :], bh(mask(d, 0)), ALU.mult).then_inc(*tick("pool", "X", l, s, d, 0))
                        pool.wait_ge(*done("X", l, s, d, 0))
                        if s:
                            pool.wait_ge(*done("pe", ("Y", l, s - 1, d)))
                        pool.tensor_tensor(b["Pm"][:, :, :], bh(ident), b["X"][:, :, :], ALU.subtract).then_inc(*tick("pool", "P", l, s, d, 0))
                        if s:
                            pool.wait_ge(*done("pe", ("KS", l, s - 1, d)))
                        pool.tensor_tensor(b["Kg"][:, :, :], kT[:, :, cc], b["EG"][:, :, :], ALU.mult).then_inc(*tick("pool", "Kg", l, s, d))
                        if live:
                            if s and (l == 0 or s - 1 >= 2):
                                pool.wait_ge(*done("pe", ("O", l, s - 1, d)))
                            pool.tensor_tensor(b["Qg"][:, :, :], qT[:, :, cc], b["EG"][:, :, :], ALU.mult).then_inc(*tick("pool", "Qg", l, s, d))
                        else:
                            got[("Qg", l, s, d)] = got[("Kg", l, s, d)]
                    for lv in range(1, LEVELS):
                        for d in range(2):
                            b = db[d]
                            if lv > 1:
                                pool.wait_ge(*done("pe", ("T1", l, s, d, lv - 1)))
                            else:
                                pool.wait_ge(*done("P", l, s, d, 0))
                            pool.tensor_tensor(b["X"][:, :, :], b["AT"][:, :, :], bh(mask(d, lv)), ALU.mult).then_inc(*tick("pool", "X", l, s, d, lv))
                elif k == "scan":
                    s = it[2]
                    live = l == 0 or s >= 2
                    for d in range(2):
                        b = db[d]
                        pool.wait_ge(*done("vn", l, s, d))
                        pool.wait_ge(*done("last", l, s, d))
                        if s:
                            pool.wait_ge(*done("pe", ("U", l, s - 1, d)))
                        pool.tensor_tensor(b["vs"][:, :, :], b["vn"][:, :, :], bc(lastc[:, d, 0, :]), ALU.mult).then_inc(*tick("pool", "vs", l, s, d))
                    for d in range(2):
                        b = db[d]
                        pool.wait_ge(*done("pe", ("O", l, s, d) if live else ("KS", l, s, d)))
                        pool.tensor_tensor(b["S"][:, :, :], b["S"][:, :, :], bc(lastc[:, d, 1, :]), ALU.mult).then_inc(*tick("pool", "Se", l, s, d))
                elif k == "dout":
                    h = it[2]
                    n = ntok(l, "dz")
                    pool.wait_ge(*done("S", l, NC, 0))
                    pool.wait_ge(*done("S", l, NC, 1))
                    if h >= 2:
                        pool.wait_ge(*done("pe", ("dout", l, h - 2)))
                    pool.tensor_tensor(do[h % 2][:, 0:n], oT[:, h, 0:n], oT[:, h, 0:n], ALU.mult).then_inc(*tick("pool", "dosq", l, h))
                    ahead(units_of(it)[0])
                    lowy(1, l, h, n, do[6 + h % 2])
                elif k == "glu":
                    if it[2] == 0:
                        pool.memset(padc[:, :, :], 0.0).then_inc(*tick("pool", "padz", l))
                    for u in units_of(it):
                        ahead(u)
                elif k == "mix":
                    n_, p = it[2], it[3]
                    n = ntok(l, "gate")
                    for j, u in enumerate(units_of(it)):
                        ahead(u)
                    if n_ != 1:
                        for j in range(2):
                            d = 2 * p + j
                            pool.wait_ge(*done("gm", it, j))
                            pool.tensor_tensor(mT[:, d, 0:n], mT[:, d, 0:n], gm[:, 0:n], ALU.add).then_inc(*tick("pool", "gadd", l, n_, d))
                elif k == "z":
                    t = it[2]
                    n = ntok(l, "cz")
                    ahead(units_of(it)[0])
                    pool.wait_ge(*done("rsc", l))
                    for a, b in segs(n)[::-1]:
                        o = HALO if a else 0
                        pool.tensor_tensor(acc[:, t, a + o:b + o], acc[:, t, a + o:b + o], rsc[:, a:b], ALU.mult).then_inc(*tick("pool", *(("xnc", l, t) if a else ("xn", l, t))))
                    lowy(0, l, t, n, zt[2 + t % 2])
                elif k == "qkv":
                    h = it[2]
                    for j, kind in enumerate(("aq", "ak")):
                        ahead((kind, l, h))
                        dst = (qh, kh)[j][h % 2]
                        pool.wait_ge(*done("read", ("rot", kind, l, h), 0))
                        pool.tensor_tensor(dst[:, 0:SEQ], dst[:, 0:SEQ], cs[:, 0, :], ALU.mult).then_inc(*tick("pool", "ropc", kind, l, h))
                        pool.wait_ge(*done("ropc", kind, l, h))
                        pool.tensor_tensor(dst[:, 0:SEQ], dst[:, 0:SEQ], at1[2][:, 0:SEQ], ALU.add).then_inc(*tick("pool", "rope", kind, l, h))
                    ahead(("av", l, h))
                elif k == "aout":
                    ahead(units_of(it)[0])
                    h = it[2]
                    n = ntok(l, "az")
                    lowy(2, l, h, n, vr)
                elif k == "out":
                    for u in units_of(it):
                        ahead(u)


    return got


def _columns(a, n):
    return a.reshape(n, P).T


def layout(inp):
    f = np.float32
    arr = {}
    x = np.concatenate([np.asarray(inp["x"])[0], np.asarray(inp["ctx"])[0]], axis=0)
    arr["xT"] = np.ascontiguousarray(x.T.reshape(KT, P, TOK).transpose(1, 0, 2))
    c = np.stack([np.asarray(inp["c"])[0], np.asarray(inp["c_ctx"])], axis=1)
    arr["cT"] = np.ascontiguousarray(c.reshape(KT, P, 2).transpose(1, 0, 2))
    w_in, w_ada = np.asarray(inp["w_in"]), np.asarray(inp["w_ada"])
    w_br, w_out = np.asarray(inp["w_branch"]), np.asarray(inp["w_out"])
    ws = np.empty((len(UNITS), P, 1024), f)
    for i, u in enumerate(UNITS):
        kind, l, t = u
        if kind.startswith("branch"):
            b = w_br[l, int(kind[-1])][:, 256 * t:256 * t + 256].reshape(NT, P, 256)
        elif kind == "ada":
            b = w_ada[l][:, P * t:P * t + P].reshape(KT, P, P)
        elif kind == "wout":
            b = w_out[l][:, P * t:P * t + P].reshape(KT, P, P)
        else:
            o = IN_COL[kind] + P * t
            b = w_in[l][:, o:o + P].reshape(KT, P, P)
        ws[i] = b.transpose(1, 0, 2).reshape(P, 1024)
    arr["wstream"] = ws
    vec = np.zeros((P, DEPTH, NV), f)
    for l in range(DEPTH):
        g = {k: np.asarray(v)[l] for k, v in inp.items() if k not in ("x", "c", "ctx", "c_ctx")}
        vec[:, l, V_BADA:V_NG] = _columns(g["b_ada"], 24)
        vec[:, l, V_NG:V_CB] = _columns(g["norm_g"], KT)
        vec[:, l, V_CB:V_LG] = _columns(g["conv_b"], NT)
        vec[:, l, V_LG:V_LB] = _columns(g["conv_ln_g"], NT)
        vec[:, l, V_LB:V_CW] = _columns(g["conv_ln_b"], NT)
        for t in range(NT):
            vec[:, l, V_CW + t * CK:V_CW + (t + 1) * CK] = g["conv_w"][:, P * t:P * t + P].T
        for t in range(3 * NT):
            vec[:, l, V_DW + 3 * t:V_DW + 3 * t + 3] = g["dn_conv_w"][:, P * t:P * t + P].T
        vec[:, l, V_DNG] = g["dn_norm_g"]
        vec[0:64, l, V_QG] = vec[64:128, l, V_QG] = g["da_q_norm_g"]
        vec[0:64, l, V_KG] = vec[64:128, l, V_KG] = g["da_k_norm_g"]
        vec[:, l, V_SUB] = g["da_subln_g"]
        vec[8:16, l, V_DT] = g["dn_dt_bias"].reshape(-1)
        vec[8:16, l, V_AL] = g["dn_a_log"].reshape(-1)
    arr["vec"] = vec
    arr["lamr"] = np.ascontiguousarray(np.broadcast_to(np.asarray(inp["da_lambda"])[None], (P, DEPTH, 4, 64)))
    arr.update(shape_constants())
    return arr


def shape_constants():
    i = np.arange(P)
    con = np.zeros((P, NCON), np.float32)
    con[:, C_ID:C_ID + P] = np.eye(P)
    con[:, C_BLK:C_BLK + P] = (i[:, None] // 64) == (i[None, :] // 64)
    for m in range(P):
        if m % 64 < 32:
            con[m + 32, C_ROT + m] = -1.0
        else:
            con[m - 32, C_ROT + m] = 1.0
    con[:, C_NEG:C_NEG + P] = np.where(i[:, None] <= i[None, :], 0.0, -1e30)
    con[:, C_NEG + P:C_NEG + 2 * P] = np.where(i[:, None] >= i[None, :], 0.0, -1e30)
    for lv in range(LEVELS):
        s = 1 << lv
        same = (i[:, None] // (2 * s)) == (i[None, :] // (2 * s))
        low = same & ((i[:, None] // s) % 2 == 0) & ((i[None, :] // s) % 2 == 1)
        con[:, C_MASK + lv * P:C_MASK + (lv + 1) * P] = low
        con[:, C_MASK + (LEVELS + lv) * P:C_MASK + (LEVELS + lv + 1) * P] = low.T
    n_freq = 16
    inv = (np.float32(10000.0) ** (-np.arange(n_freq, dtype=np.float32) / np.float32(n_freq))).astype(np.float32)
    t = np.arange(SEQ)
    row, colm = (t // 64).astype(np.float32), (t % 64).astype(np.float32)
    ang = np.concatenate([row[:, None] * inv, colm[:, None] * inv], axis=-1)
    ang = np.concatenate([ang, ang], axis=-1).T
    ang = np.concatenate([ang, ang], axis=0)
    rope = np.stack([np.cos(ang), np.sin(ang)], axis=1).astype(np.float32)
    return {"con": con, "rope": rope}


_ARGS = ["wstream", "xT", "cT", "vec", "lamr", "con", "rope"]


def kernel(**inputs):
    import concourse.bacc as _bacc
    from concourse import mybir as _mybir
    from concourse.bass_utils import run_bass_kernel_spmd as _run

    arrays = layout(inputs)

    def program(steps):
        nc = _bacc.Bacc("TRN2", target_bir_lowering=False, num_devices=1)
        args = [nc.dram_tensor(n, arrays[n].shape, _mybir.dt.float32, kind="ExternalInput").ap() for n in _ARGS]
        args.append(nc.dram_tensor("outT", (P, KT, SEQ), _mybir.dt.float32, kind="ExternalOutput").ap())
        return nc, build(nc, *args, steps)

    _, steps = program({})
    nc, _ = program(steps)
    r = _run(nc, [arrays], core_ids=[0])
    out = r.results[0]["outT"]
    return np.ascontiguousarray(out.transpose(2, 1, 0)).reshape(1, SEQ, D)
```

```python
import math
from contextlib import ExitStack

import numpy as np

import concourse.bass as bass
from concourse import mybir

F32 = mybir.dt.float32
F32R = mybir.dt.float32r
ACT = mybir.ActivationFunctionType
ALU = mybir.AluOpType
AX_X = mybir.AxisListType.X

P = 128
D = 1024
KT = D // P
BW = 512
NT = BW // P
SEQ, CTX = 512, 256
TOK = SEQ + CTX
NC = TOK // P
DEPTH = 2
CK = 31
HALO = CK // 2
PADW = HALO + SEQ + HALO + CTX + HALO
ACCW = SEQ + HALO + CTX
LEVELS = 7
ORDER = ((4, 5, 0, 1, 2, 3), (5, 4, 3, 2, 1, 0))
RMS_EPS, LN_EPS = 1e-6, 1e-5
V_BADA, V_NG, V_CB, V_LG, V_LB = 0, 24, 32, 36, 40
V_CW = 44
V_DW = V_CW + NT * CK
V_DNG = V_DW + 3 * NT * 3
V_QG, V_KG, V_SUB, V_DT, V_AL = (V_DNG + i for i in range(1, 6))
NV = V_AL + 1
C_ID, C_BLK, C_ROT, C_NEG, C_MASK = 0, 128, 256, 384, 640
NCON = C_MASK + 2 * LEVELS * P


def ntok(l, kind):
    return TOK if l == 0 or kind in ("dk", "dv", "gb", "ak", "av") else SEQ


def segs(n):
    return [(0, SEQ), (SEQ, TOK)] if n == TOK else [(0, n)]


def weave(a, b):
    out, j = [], 0
    for i, x in enumerate(a):
        out.append(x)
        k = (i + 1) * len(b) // len(a)
        out += b[j:k]
        j = k
    return out + b[j:]


def merge_steps(l, n):
    out = []
    for p in range(4):
        out += [("gate", l, n, 2 * p), ("gate", l, n, 2 * p + 1), ("branch", l, n, p)]
    return out


def schedule():
    out = [("ada", 0, m) for m in range(3)] + [("nsum", 0)] + [("ada", 0, m) for m in range(3, 16)]
    for l in range(DEPTH):
        if l:
            out.append(("nsum", l))
        out += [("nh", l), ("gb", l)]
        for h in range(NT):
            out.append(("dqkv", l, h, "dk"))
            out += [("dsq", l, h - 1)] * (h > 0)
            out.append(("dqkv", l, h, "dv"))
            out += [("dsum", l, h - 1)] * (h > 0) + [("gturn", l)] * (h == 0)
            out.append(("dqkv", l, h, "dq"))
            out += [("dturn", l, h - 1)] * (h > 0)
        out += [("dsq", l, NT - 1), ("dsum", l, NT - 1), ("dturn", l, NT - 1)]
        for s in range(NC):
            out += [("prep", l, s), ("scan", l, s)]
        out += [("dout", l, h) for h in range(NT)]
        out += [("glu", l, t) for t in range(NT)]
        out += merge_steps(l, 1)
        out += [("ln", l)]
        out += [("z", l, t) for t in range(NT)]
        heads = [[("qunit", l, h, "aq"), ("qsum", l, h, "aq"), ("qrot", l, h, "aq"),
                  ("qunit", l, h, "ak"), ("qsum", l, h, "ak"), ("qrot", l, h, "ak"),
                  ("vunit", l, h), ("vturn", l, h)] for h in range(NT)]
        att = [[("att", l, h, qt) for qt in range(ntok(l, "aq") // P)] for h in range(NT)]
        fill = merge_steps(l, 0)
        late = [("ada", 0, m) for m in range(16, 24)] + [("ada", 1, m) for m in range(24)] if l == 0 else []
        mid = weave(heads[0], fill[:8])
        mid += weave(att[0], weave(heads[1], fill[8:]))
        mid += [("aout", l, 0)]
        for h in (1, 2):
            mid += weave(att[h], heads[h + 1]) + [("aout", l, h)]
        mid += weave(att[3], [("gate", l, 2, 0), ("gate", l, 2, 1)]) + [("aout", l, 3)] + merge_steps(l, 2)[2:]
        out += weave(mid, late)
        out += [("out", l)]
    return out


def units_of(item):
    k, l = item[0], item[1]
    if k == "ada":
        return [("ada", l, item[2])]
    if k == "gb":
        return [("gb", l, 0)]
    if k in ("dqkv", "qunit"):
        return [(item[3], l, item[2])]
    if k == "vunit":
        return [("av", l, item[2])]
    if k == "dout":
        return [("dz", l, item[2])]
    if k == "glu":
        return [("val", l, item[2]), ("glu", l, item[2])]
    if k == "z":
        return [("cz", l, item[2])]
    if k in ("gate", "branch"):
        return [("%s%d" % (k, item[2]), l, item[3])]
    if k == "aout":
        return [("az", l, item[2])]
    if k == "out":
        return [("wout", l, d) for d in range(KT)]
    return []


def low_on_vector(u):
    return u[0] == "ada" and u[1] == 0 and u[2] < 16


ITEMS = schedule()
UNITS = [u for it in ITEMS for u in units_of(it)]
WIDX = {u: i for i, u in enumerate(UNITS)}
IN_COL = {"val": 0, "glu": 512, "cz": 1024, "dq": 1536, "dk": 2048, "dv": 2560, "dz": 3072, "gb": 3584,
          "aq": 3600, "ak": 4112, "av": 4624, "az": 5136, "gate0": 5648, "gate1": 6672, "gate2": 7696}


def build(nc, wstream, xT, cT, vec, lamr, con, rope, outT, steps):
    first_pass = not steps
    got = {}
    with ExitStack() as ctx:
        base = (nc.sbuf_base + 63) // 64 * 64
        pos = [base]

        def at(name, shape, dt=F32, off=None):
            n = 4 * int(np.prod(shape[1:]))
            if off is None:
                off = pos[0]
                pos[0] += (n + 31) // 32 * 32
            return nc.alloc_sbuf_tensor_at(name, shape, dt, offset=off)

        stages = ["start"] + sorted({it[0] for it in ITEMS})
        names = ["%s_%s" % (e, k) for e in ("pe", "act", "dve", "pool") for k in stages]
        names += ["w_high", "w_low_pool", "w_low_dve", "raw0", "raw1", "raw2", "small_in", "x_in", "x_out", "rope_in"]
        sem = {n: ctx.enter_context(nc.semaphore(n)) for n in names}
        count = {n: 0 for n in sem}
        stage = ["start"]

        def tick(name, *key, by=1):
            name = {"hi": "w_high", "lo": "w_low_" + name}.get(key[0], name)
            if name not in sem:
                name += "_" + stage[0]
            count[name] += by
            got[key] = (name, count[name])
            return sem[name], by

        def done(*key):
            assert first_pass or key in steps, key
            name, value = steps.get(key, ("x_in", 1))
            return sem[name], value

        hH = at("hH", [P, KT, TOK], F32R)
        hL = at("hL", [P, KT, TOK], F32R)
        raw = [at("raw%d" % i, [P, 1024]) for i in range(3)]
        wH = [at("wH%d" % i, [P, 1024], F32R) for i in range(3)]
        wL = [at("wL%d" % i, [P, 1024], F32R) for i in range(3)]
        cons = at("cons", [P, NCON])
        ones = at("ones", [P, P])
        vecs = at("vecs", [P, DEPTH, NV])
        csx = at("csx", [P, KT * 4 + P - 4], F32R)
        csx4 = csx[:, 0:KT * 4].rearrange("p (k c) -> p k c", c=4)
        adar = at("adar", [4, P])
        ada = at("ada", [P, DEPTH, 24, 2])
        gs = at("gs", [P, DEPTH, KT, 2])
        misc = at("misc", [P, 16])
        lam_dot = at("lam_dot", [P, DEPTH, 2])
        lam_exp = at("lam_exp", [P, DEPTH, 2])
        gcol = at("gcol", [P, 2, NC, 16])
        bcol = at("bcol", [P, NC, 16])
        stat = at("stat", [P, 2, 8])
        c1 = at("c1", [P, 2])
        lastc = at("lastc", [P, 2, 2, NT])
        eps = misc[:, 0:1]
        lneps = misc[:, 1:2]
        nega = misc[:, 2:4]
        nlam = misc[:, 4:6]
        qg8 = misc[:, 6:8]
        sub1 = misc[:, 8:10]
        pos[0] = (pos[0] + 63) // 64 * 64
        A0 = pos[0]
        AEND = A0 + (nc.sbuf_usable_end - A0) // 32 * 32
        ident = cons[:, C_ID:C_ID + P]
        blk = cons[:, C_BLK:C_BLK + P]
        rot = cons[:, C_ROT:C_ROT + P]

        def neg(d):
            return cons[:, C_NEG + d * P:C_NEG + (d + 1) * P]

        def mask(d, lv):
            o = C_MASK + (d * LEVELS + lv) * P
            return cons[:, o:o + P]

        T3 = 4 * TOK
        assert AEND - A0 >= 111616, 111616 - AEND + A0
        def arena(name, shape, off, dt=F32):
            assert A0 + off + 4 * int(np.prod(shape[1:])) <= AEND, (name, A0 + off, AEND)
            return at(name, shape, dt, A0 + off)

        qT = arena("qT", [P, NT, TOK], 0)
        kT = arena("kT", [P, NT, TOK], 4 * T3)
        Ktm = arena("Ktm", [P, NC, NT, P], 8 * T3)
        Vtm = arena("Vtm", [P, NC, NT, P], 12 * T3)
        oT = arena("oT", [P, NT, TOK], 16 * T3)
        B0 = 20 * T3
        names = ("Pm", "intra", "Kg", "Qg", "E", "EG", "AT", "X", "S", "vn", "vs")
        db = [{n: arena("%s%d" % (n, d), [P, NT, P], B0 + (d * len(names) + i) * 4 * BW)
               for i, n in enumerate(names)} for d in range(2)]
        GR = arena("GR", [48, TOK], B0 + 2 * len(names) * 4 * BW)
        pad3 = [arena("pad3_%d" % i, [P, TOK + 3], B0 + i * (T3 + 32)) for i in range(2)]
        c3 = [arena("c3_%d" % i, [P, TOK + 1], B0 + 2 * T3 + 64 + i * (T3 + 32)) for i in range(2)]
        vb = [arena("vb_%d" % i, [P, TOK], B0 + 4 * T3 + 128 + i * T3) for i in range(2)]
        sqd = [arena("sqd_%d" % i, [P, TOK], B0 + 6 * T3 + 128 + i * T3) for i in range(2)]
        rsd = [arena("rsd_%d" % i, [P, TOK], B0 + 8 * T3 + 128 + i * T3) for i in range(2)]
        gbt = [arena("gbt_%d" % i, [16, TOK], B0 + (10 + i) * T3 + 128) for i in range(4)]
        xs = arena("xs", [P, KT, TOK], 8 * T3)
        sqn = [arena("sqn_%d" % i, [P, TOK], (16 + i) * T3) for i in range(2)]
        rsn = arena("rsn", [P, TOK], 18 * T3)
        hn = [arena("hn_%d" % i, [P, TOK], (19 + i) * T3) for i in range(2)]
        mT = arena("mT", [P, KT, TOK], 0)
        yH = arena("yH", [P, NT, TOK], 8 * T3, F32R)
        yL = arena("yL", [P, NT, TOK], 12 * T3, F32R)
        CW = (4 * PADW * NT + 31) // 32 * 32
        GT = CW + 4 * ACCW * NT
        sg = [arena("sg%d" % i, [P, TOK], AEND - A0 - (3 - i) * T3) for i in range(2)]
        gm = arena("gm", [P, TOK], AEND - A0 - T3)
        do = [arena("do_%d" % i, [P, TOK], (20 + i) * T3) for i in range(10)]
        padc = arena("padc", [P, NT, PADW], 16 * T3)
        acc = arena("acc", [P, NT, ACCW], 16 * T3 + CW)
        CZ = (16 * T3 + GT + 31) // 32 * 32
        gl = [arena("gl_%d" % i, [P, TOK], CZ + i * T3) for i in range(2)]
        sqc = [arena("sqc_%d" % i, [P, ACCW], 16 * T3 + i * 3264) for i in range(2)]
        rsc = arena("rsc", [P, TOK], CZ)
        zt = [arena("zt_%d" % i, [P, TOK], 16 * T3 + i * T3) for i in range(4)]
        qh = [arena("qh_%d" % i, [P, TOK], (16 + i) * T3) for i in range(2)]
        kh = [arena("kh_%d" % i, [P, TOK], (18 + i) * T3) for i in range(2)]
        Va = [arena("Va_%d" % i, [P, NC, P], (20 + i) * T3) for i in range(2)]
        vr = arena("vr", [P, TOK], 22 * T3)
        at1 = [arena("at1_%d" % i, [P, TOK], (23 + i) * T3) for i in range(3)]
        Pa = [[arena("Pa_%d%d" % (i, m), [P, TOK], (26 + 2 * i + m) * T3) for m in range(2)] for i in range(2)]
        aT = [arena("aT_%d" % i, [P, NC, P], (30 + i) * T3) for i in range(2)]
        cs = arena("cs", [P, 2, SEQ], 32 * T3)
        lamt = arena("lamt", [P, DEPTH, 4, 64], 30 * T3)
        lamp = arena("lamp", [P, DEPTH, 2, 64], 31 * T3)
        csb = arena("csb", [P, KT, 2], 31 * T3 + 1024)
        cs32 = arena("cs32", [P, KT, 2], 31 * T3 + 1088)

        xscr = nc.dram_tensor("x_between", (P, KT, TOK), F32, kind="Internal").ap()

        banks = ctx.enter_context(nc.psum_tensor("banks", [P, 8, 512], F32))
        bank_user = [None] * 8
        bank_next = [0]
        place = {}
        readers = {}

        def product(pe, key, width):
            n = 2 if width > 512 else 1
            b = bank_next[0]
            if n == 2 and b % 2:
                b += 1
            b %= 8
            bank_next[0] = (b + n) % 8
            for i in range(b, b + n):
                if bank_user[i] is not None and (i == b or bank_user[i] != bank_user[i - 1]):
                    last = 1 if ("read", bank_user[i], 1) in steps else 0
                    pe.wait_ge(*done("read", bank_user[i], last))
            for i in range(b, b + n):
                bank_user[i] = key
            place[key] = banks[:, b:b + n, :].rearrange("p b n -> p (b n)")
            return place[key]

        def tick_read(eng, key):
            r = readers.get(key, 0)
            readers[key] = r + 1
            return tick(eng, "read", key, r)

        def bc(ap, n=P):
            return ap.unsqueeze(2).to_broadcast([ap.shape[0], ap.shape[1], n])

        def v4(ap):
            return ap[:, 0:4 * P].rearrange("p (h c) -> p h c", h=4)

        def bh(ap):
            return ap.unsqueeze(1).to_broadcast([P, NT, P])

        def fresh(ap, d, lv):
            return ap.rearrange("p h (b two s) -> p (h b) two s", two=2, s=1 << lv)[:, :, 1 - d, :]

        mixes = [it for it in ITEMS if it[0] == "mix"]

        def lowh(l, t):
            dve = nc.vector
            for p, (a, b) in enumerate(segs(TOK)):
                dve.wait_ge(*done("hH", l, t, p))
                dve.scalar_tensor_tensor(hL[:, t, a:b], hn[t % 2][:, a:b], ada[:, l, t, p:p + 1],
                                              hH[:, t, a:b].bitcast(F32), ALU.add, ALU.subtract).then_inc(
                                                  *tick("dve", "h" if p else "hl0", l, t))

        def ocopy(l, h, qt):
            dve = nc.vector
            key = ("o", l, h, qt)
            dve.wait_ge(*done("pe", key))
            if qt == 0 and h:
                dve.wait_ge(*done("ao", l, h - 1))
            ins = dve.tensor_copy(at1[2][:, qt * P:(qt + 1) * P], place[key][:, 0:P])
            ins.then_inc(*tick_read("dve", key))
            got[("ocopy", l, h, qt)] = got[("read", key, 0)]

        block = ctx.enter_context(nc.Block())

        @block.tensor
        def _(pe):
            stage[0] = "start"
            def dense(u, out, movH, movL, n, kts, col0=0, width=P):
                i = WIDX[u] % 3
                pe.wait_ge(*done("hi", u))
                pe.wait_ge(*done("lo", u))
                for kt in range(kts):
                    lo = kt * width + col0
                    H, L = wH[i][:, lo:lo + P], wL[i][:, lo:lo + P]
                    for j, (w, m) in enumerate(((H, movH), (H, movL), (L, movH))):
                        for a, b in n:
                            last = pe.matmul(out[:, a:b], w, m[:, kt, a:b], start=(kt == 0 and j == 0),
                                             stop=(kt == kts - 1 and j == 2))
                return last

            def unit(u, kind):
                out = product(pe, u, ntok(u[1], kind))
                pe.wait_ge(*done("h", u[1], KT - 1))
                last = dense(u, out, hH, hL, segs(ntok(u[1], kind)), KT)
                last.then_inc(*tick("pe", "pe", u))

            def allsum(key, stat_ap, tiles, n, dep, kt_n):
                out = product(pe, key, n)
                for t in range(kt_n):
                    pe.wait_ge(*done(*dep(t)))
                    for a, b in segs(n):
                        last = pe.matmul(out[:, a:b], stat_ap, tiles(t, a, b), start=(t == 0), stop=(t == kt_n - 1))
                    last.then_inc(*(tick("pe", "pe", key) if t == kt_n - 1 else tick("pe", "pe", key, t)))

            def turn(key, src, n, dep):
                out = product(pe, key, n)
                pe.wait_ge(*done(*dep))
                for c in range(n // P):
                    last = pe.transpose(out[:, c * P:(c + 1) * P], src[:, c * P:(c + 1) * P], ident)
                last.then_inc(*tick("pe", "pe", key))

            def heads(key, f, *deps, parts=1):
                out = product(pe, key, 512)
                for dep in deps:
                    pe.wait_ge(*done(*dep))
                for h in range(NT):
                    for j in range(parts):
                        l, r = f(h, j)
                        last = pe.matmul(out[:, h * P:(h + 1) * P], l, r, start=(j == 0), stop=(j == parts - 1))
                last.then_inc(*tick("pe", "pe", key))

            def scores(l, h, qt):
                keys = segs(TOK) if qt < 4 else [(SEQ, TOK)]
                q_, k_ = qh[h % 2], kh[h % 2]
                for m in range(2):
                    key = ("sc", l, h, qt, m)
                    out = product(pe, key, TOK)
                    pe.wait_ge(*done("rope", "aq", l, h))
                    pe.wait_ge(*done("rope", "ak", l, h))
                    r = slice(64 * m, 64 * m + 64)
                    o = 0
                    for a, b in keys:
                        last = pe.matmul(out[:, o:o + b - a], q_[r, qt * P:(qt + 1) * P], k_[r, a:b],
                                         start=True, stop=True)
                        o += b - a
                    last.then_inc(*tick("pe", "pe", key))

            def values(l, h, qt):
                n = NC if qt < 4 else CTX // P
                key = ("o", l, h, qt)
                out = product(pe, key, P)
                pe.wait_ge(*done("aT", l, h, qt))
                pe.wait_ge(*done("Va", l, h))
                for c in range(n):
                    last = pe.matmul(out[:, 0:P], Va[h % 2][:, NC - n + c, :], aT[qt % 2][:, c, :],
                                     start=(c == 0), stop=(c == n - 1))
                last.then_inc(*tick("pe", "pe", key))

            def decay(l, s):
                for d in range(2):
                    cc = slice(ORDER[d][s] * P, (ORDER[d][s] + 1) * P)
                    r0 = 32 * d
                    c = r0 + 8 + 4 * d
                    heads(("G", l, s, d), lambda h, j: (ident[r0:r0 + 16, c + h:c + h + 1].to_broadcast([16, P]),
                                                        GR[r0:r0 + 16, cc]), ("cum", l, d))

            turning = []

            def ada_turn():
                if turning:
                    u = turning.pop()
                    key = ("adaT",) + u[1:]
                    out = product(pe, key, 4)
                    pe.wait_ge(*done("arow", *u[1:]))
                    pe.transpose(out[:, 0:4], adar[0:4, :], ident[0:4, 0:4]).then_inc(*tick("pe", "pe", key))

            pe.wait_ge(*done("ones"))
            pe.wait_ge(*done("con_in"))
            for it in ITEMS:
                stage[0], k, l = it[0], it[0], it[1]
                if k == "ada":
                    m = it[2]
                    u = ("ada", l, m)
                    out = product(pe, u, P)
                    pe.wait_ge(*done("csL"))
                    if l == 0 and m == 0:
                        pe.wait_ge(*done("csx0"))
                    pe.wait_ge(*done("hi", u))
                    pe.wait_ge(*done("lo", u))
                    i = WIDX[u] % 3
                    for kt in range(KT):
                        for j, w in enumerate((wH, wL)):
                            last = pe.matmul(out[:, 0:P], csx[:, 4 * kt:4 * kt + P],
                                             w[i][:, kt * P:(kt + 1) * P], start=(kt == 0 and j == 0),
                                             stop=(kt == KT - 1 and j == 1))
                    last.then_inc(*tick("pe", "pe", u))
                    ada_turn()
                    turning.append(u)
                    if m == 15 and l == 0 or m == 23 and l == 1:
                        ada_turn()
                elif k == "nsum":
                    allsum(it, ones[:, :], lambda t, a, b: sqn[t % 2][:, a:b], TOK, lambda t: ("sqn", l, t), KT)
                elif k == "gb":
                    unit(units_of(it)[0], "gb")
                elif k == "gturn":
                    out = product(pe, ("gturn", l), 1024)
                    pe.wait_ge(*done("cum", l, 0))
                    pe.wait_ge(*done("cum", l, 1))
                    pe.wait_ge(*done("beta", l))
                    for j in range(3):
                        src = (GR[0:16, :], GR[32:48, :], gbt[0][:, :])[j]
                        idn = ident[32:48, 32:48] if j == 1 else ident[0:16, 0:16]
                        for c in range(NC):
                            o = (0, 512, NC * 16)[j] + c * 16
                            last = pe.transpose(out[:, o:o + 16], src[:, c * P:(c + 1) * P], idn)
                    last.then_inc(*tick("pe", "pe", ("gturn", l)))
                elif k == "dqkv":
                    h, kind = it[2], it[3]
                    unit((kind, l, h), kind)
                    if kind == "dv":
                        turn(("vturn", l, h), vb[h % 2], TOK, ("silu", "dv", l, h))
                elif k == "dsum":
                    h = it[2]
                    for i, kind in enumerate(("dk", "dq")):
                        allsum(("dss", kind, l, h), ones[:, :], lambda t, a, b: sqd[i][:, a:b], ntok(l, kind),
                               lambda t: ("sqd", kind, l, h), 1)
                elif k == "dturn":
                    h = it[2]
                    turn(("kturn", l, h), kT[:, h, :], TOK, ("dn", "dk", l, h))
                elif k == "prep":
                    s = it[2]
                    live = l == 0 or s >= 2
                    if s == 0:
                        decay(l, s)
                    for d in range(2):
                        cc = slice(ORDER[d][s] * P, (ORDER[d][s] + 1) * P)
                        heads(("KK", l, s, d), lambda h, j: (kT[:, h, cc], kT[:, h, cc]), ("dn", "dk", l, 3))
                    if live:
                        for d in range(2):
                            cc = slice(ORDER[d][s] * P, (ORDER[d][s] + 1) * P)
                            heads(("QK", l, s, d), lambda h, j: (kT[:, h, cc], qT[:, h, cc]), ("dn", "dq", l, 3))
                    for lv in range(LEVELS):
                        if lv > 0:
                            for d in range(2):
                                b = db[d]
                                heads(("T1", l, s, d, lv), lambda h, j: (b["X"][:, h, :], b["vs"][:, h, :]),
                                      ("X", l, s, d, lv), ("M", l, s, d, lv - 1))
                            for d in range(2):
                                b = db[d]
                                key = ("PU", l, s, d, lv)
                                out = product(pe, key, 256)
                                pe.wait_ge(*done("T1", l, s, d, lv))
                                for h in range(NT):
                                    last = pe.matmul(out[:, 64 * h:64 * h + 64], b["E"][:, h, :],
                                                     fresh(b["Pm"][:, h:h + 1, :], d, lv), start=True, stop=True)
                                last.then_inc(*tick("pe", "pe", key))
                        if lv < LEVELS - 1:
                            for d in range(2):
                                out = product(pe, ("MT", l, s, d, lv), 512)
                                pe.wait_ge(*done("P", l, s, d, lv))
                                for h in range(NT):
                                    last = pe.transpose(out[:, h * P:(h + 1) * P], db[d]["Pm"][:, h, :], ident)
                                last.then_inc(*tick("pe", "pe", ("MT", l, s, d, lv)))
                elif k == "scan":
                    s = it[2]
                    live = l == 0 or s >= 2
                    for d in range(2):
                        b = db[d]
                        heads(("KS", l, s, d), lambda h, j: (b["Kg"][:, h, :], b["S"][:, h, :]),
                              ("Kg", l, s, d), ("S", l, s, d))
                    if s + 1 < NC:
                        decay(l, s + 1)
                    for d in range(2):
                        b = db[d]
                        heads(("Y", l, s, d), lambda h, j: (b["Pm"][:, h, :], b["vn"][:, h, :]),
                              ("R", l, s, d), ("P", l, s, d, LEVELS - 1))
                    for d in range(2):
                        b = db[d]
                        if live:
                            heads(("O", l, s, d), lambda h, j: ((b["S"][:, h, :], b["Qg"][:, h, :]) if j == 0 else
                                                                (b["vn"][:, h, :], b["intra"][:, h, :])),
                                  ("Qg", l, s, d), ("vn", l, s, d), ("intra", l, s, d), parts=2)
                    for d in range(2):
                        b = db[d]
                        ch = ORDER[d][s]
                        heads(("U", l, s, d), lambda h, j: (Ktm[:, ch, h, :], b["vs"][:, h, :]), ("vs", l, s, d))
                elif k == "dout":
                    h = it[2]
                    n = ntok(l, "dz")
                    unit(("dz", l, h), "dz")
                    allsum(it, ones[:, :], lambda t, a, b: do[h % 2][:, a:b], n, lambda t: ("dosq", l, h), 1)
                elif k == "glu":
                    unit(("val", l, it[2]), "val")
                    unit(("glu", l, it[2]), "glu")
                elif k == "gate":
                    unit(units_of(it)[0], "gate")
                elif k == "branch":
                    n, p = it[2], it[3]
                    u = ("branch%d" % n, l, p)
                    w = ntok(l, "gate")
                    for j in range(2):
                        out = product(pe, (u, j), w)
                        pe.wait_ge(*done("y", n, l, NT - 1))
                        last = dense(u, out, yH, yL, segs(w), NT, j * P, 2 * P)
                        last.then_inc(*tick("pe", "pe", (u, j)))
                    got[("pe", u)] = got[("pe", (u, 1))]
                elif k == "ln":
                    n = ntok(l, "cz")
                    allsum(("lnsum", l), ones[:, :], lambda t, a, b: acc[:, t, a + (HALO if a else 0):b + (HALO if a else 0)],
                           n, lambda t: ("conv", l, t), NT)
                    allsum(("lnvar", l), ones[:, :], lambda t, a, b: sqc[t % 2][:, a + (HALO if a else 0):b + (HALO if a else 0)],
                           n, lambda t: ("sqc", l, t), NT)
                elif k == "z":
                    unit(("cz", l, it[2]), "cz")
                elif k == "qunit":
                    unit((it[3], l, it[2]), it[3])
                elif k == "qsum":
                    h, kind = it[2], it[3]
                    allsum(("ss", kind, l, h), blk, lambda t, a, b: at1[0][:, a:b], ntok(l, kind),
                           lambda t: ("asq", kind, l, h), 1)
                elif k == "qrot":
                    h, kind = it[2], it[3]
                    dst = (qh if kind == "aq" else kh)[h % 2]
                    out = product(pe, ("rot", kind, l, h), SEQ)
                    pe.wait_ge(*done("an", kind, l, h))
                    pe.matmul(out[:, 0:SEQ], rot, dst[:, 0:SEQ], start=True,
                              stop=True).then_inc(*tick("pe", "pe", ("rot", kind, l, h)))
                elif k == "vunit":
                    unit(("av", l, it[2]), "av")
                elif k == "vturn":
                    turn(("aturn", l, it[2]), vr, TOK, ("vr", l, it[2]))
                elif k == "att":
                    h, qt = it[2], it[3]
                    nq = ntok(l, "aq") // P
                    if qt == 0:
                        scores(l, h, 0)
                    if qt + 1 < nq:
                        scores(l, h, qt + 1)
                    n = NC if qt < 4 else CTX // P
                    turn(("pt", l, h, qt), Pa[qt % 2][0], n * P, ("mixp", l, h, qt))
                    if qt:
                        values(l, h, qt - 1)
                    if qt == nq - 1:
                        values(l, h, qt)
                elif k == "aout":
                    h = it[2]
                    n = ntok(l, "az")
                    unit(("az", l, h), "az")
                    allsum(("oss", l, h), ones[:, :], lambda t, a, b: at1[0][:, a:b], n, lambda t: ("aosq", l, h), 1)
                elif k == "out":
                    w = ntok(l, "wout")
                    for u in units_of(it):
                        out = product(pe, u, w)
                        pe.wait_ge(*done("m", l, KT - 1))
                        last = dense(u, out, hH, hL, segs(w), KT)
                        last.then_inc(*tick("pe", "pe", u))

        @block.sync
        def _(sp):
            stage[0] = "start"
            sp.dma_start(cons[:, :], con).then_inc(*tick("small_in", "con_", by=16))
            sp.dma_start(vecs[:, :, :], vec).then_inc(*tick("small_in", "vec_", by=16))
            sp.dma_start(csb[:, :, :], cT).then_inc(*tick("small_in", "c_", by=16))
            sp.dma_start(lamt[:, :, :, :], lamr).then_inc(*tick("small_in", "con_in", by=16))

            for w, u in enumerate(UNITS):
                i = w % 3
                if w == 3:
                    sp.dma_start(xs[:, :, :], xT).then_inc(*tick("x_in", "x_in", 0, by=16))
                if w >= 3:
                    sp.wait_ge(*done("lo", UNITS[w - 3]))
                sp.dma_start(raw[i][:, :], wstream[w]).then_inc(*tick("raw%d" % i, "raw", u, by=16))

        @block.scalar
        def _(act):
            stage[0] = "start"
            done_hi = [0]
            prev_ada = []
            last_sg = [None, None]

            def ahead(u):
                while done_hi[0] < min(WIDX[u] + 3, len(UNITS)):
                    w = done_hi[0]
                    v = UNITS[w]
                    act.wait_ge(*done("raw", v))
                    if w >= 3:
                        act.wait_ge(*done("pe", UNITS[w - 3]))
                        act.wait_ge(*done("lo", UNITS[w - 3]))
                    act.activation(wH[w % 3][:, :], raw[w % 3][:, :], ACT.Copy).then_inc(*tick("act", "hi", v))
                    done_hi[0] += 1

            def rsqrt(src, dst, scale, e, key, readkey, n):
                act.wait_ge(*done("pe", readkey))
                ins = act.activation(dst[:, 0:n], place[readkey][:, 0:n], ACT.Ln, bias=e, scale=scale)
                ins.then_inc(*tick_read("act", readkey))
                act.wait_ge(*done("read", readkey, readers[readkey] - 1))
                act.activation(dst[:, 0:n], dst[:, 0:n], ACT.Exp, scale=-0.5).then_inc(*tick("act", *key))

            def soft(l, h, qt):
                w = TOK if qt < 4 else CTX
                nq = ntok(l, "aq") // P
                i = qt % 2
                for m in range(2):
                    key = ("sc", l, h, qt, m)
                    act.wait_ge(*done("nmx", l, h, qt))
                    if qt >= 2:
                        act.wait_ge(*done("pe", ("pt", l, h, qt - 2)))
                    elif h:
                        act.wait_ge(*done("pe", ("pt", l, h - 1, nq - 2 + i)))
                    act.activation(Pa[i][m][:, 0:w], place[key][:, 0:w], ACT.Exp, bias=stat[:, i, 2 + m:3 + m],
                                   accum_out=stat[:, i, 4 + m:5 + m]).then_inc(*tick_read("act", key))

            def decay(l, s):
                for d in range(2):
                    b = db[d]
                    g = ("G", l, s, d)
                    act.wait_ge(*done("pe", g))
                    if s:
                        act.wait_ge(*done("last", l, s - 1, d))
                        act.wait_ge(*done("Kg", l, s - 1, d))
                        act.wait_ge(*done("Qg", l, s - 1, d))
                    else:
                        act.wait_ge(*done("prepfree", l))
                    act.activation(b["EG"][:, :, :], v4(place[g]), ACT.Exp).then_inc(*tick_read("act", g))
                for d in range(2):
                    b = db[d]
                    act.wait_ge(*done("E", l, s, d))
                    act.activation(b["E"][:, :, :], b["E"][:, :, :], ACT.Exp).then_inc(*tick("act", "DT", l, s, d))

            act.wait_ge(*done("con_in"))
            act.wait_ge(*done("misc"))
            act.activation(cs32[:, :, :], csb[:, :, :], ACT.Silu).then_inc(*tick("act", "cs32"))
            act.wait_ge(*done("cs32"))
            act.activation(csx4[:, :, 0:2], cs32[:, :, :], ACT.Copy).then_inc(*tick("act", "csH"))
            for l in range(DEPTH):
                act.activation(nega[:, l:l + 1], vecs[:, l, V_AL:V_AL + 1], ACT.Exp).then_inc(*tick("act", "aexp", l))
            act.wait_ge(*done("lamdot"))
            act.activation(lam_exp[:, :, :], lam_dot[:, :, :], ACT.Exp).then_inc(*tick("act", "lamexp"))

            for it in ITEMS:
                stage[0], k, l = it[0], it[0], it[1]
                if k == "ada":
                    u = ("ada", l, it[2])
                    ahead(u)
                    act.wait_ge(*done("pe", u))
                    if prev_ada:
                        act.wait_ge(*done("pe", ("adaT",) + prev_ada[-1][1:]))
                    prev_ada.append(u)
                    act.activation(adar[0:4, :], place[u][0:4, 0:P], ACT.Copy).then_inc(*tick_read("act", u))
                    got[("arow",) + u[1:]] = got[("read", u, 0)]
                elif k == "nsum":
                    act.wait_ge(*(done("x_in", 0) if l == 0 else done("xnew", l - 1, KT - 1)))
                    for t in range(KT):
                        if t >= 2:
                            act.wait_ge(*done("pe", it, t - 2))
                        act.activation(sqn[t % 2][:, :], xs[:, t, :], ACT.Square).then_inc(*tick("act", "sqn", l, t))
                    rsqrt(None, rsn, 1.0 / D, eps, ("rsn", l), it, TOK)
                elif k == "nh":
                    for t in range(KT):
                        for p, (a, b) in enumerate(segs(TOK)):
                            act.wait_ge(*done("hn", l, t, p))
                            act.activation(hH[:, t, a:b], hn[t % 2][:, a:b], ACT.Identity,
                                             bias=ada[:, l, t, p:p + 1]).then_inc(*tick("act", "hH", l, t, p))
                elif k == "gb":
                    u = units_of(it)[0]
                    ahead(u)
                    act.wait_ge(*done("pe", u))
                    act.wait_ge(*done("h", l, KT - 1))
                    ps = place[u]
                    act.activation(gbt[0][:, :], ps[0:16, 0:TOK], ACT.Sigmoid).then_inc(*tick("act", "beta", l))
                    act.activation(gbt[1][:, :], ps[0:16, 0:TOK], ACT.Identity,
                                        bias=vecs[0:16, l, V_DT:V_DT + 1]).then_inc(*tick_read("act", u))
                    act.wait_ge(*done("read", u, 0))
                    act.activation(gbt[2][:, :], gbt[1][:, :], ACT.Abs).then_inc(*tick("act", "gabs", l))
                    act.wait_ge(*done("gabs", l))
                    act.activation(gbt[2][:, :], gbt[2][:, :], ACT.Exp, scale=-1.0).then_inc(*tick("act", "gexp", l))
                    act.wait_ge(*done("gexp", l))
                    act.activation(gbt[2][:, :], gbt[2][:, :], ACT.Ln, bias=1.0).then_inc(*tick("act", "gln", l))
                elif k == "dqkv":
                    h, kind = it[2], it[3]
                    u = (kind, l, h)
                    ahead(u)
                    n = ntok(l, kind)
                    i = (3 * h + ("dk", "dv", "dq").index(kind)) % 2
                    act.wait_ge(*done("pe", u))
                    act.wait_ge(*done("pad0", l))
                    if 3 * h + ("dk", "dv", "dq").index(kind) >= 2:
                        act.wait_ge(*done("c3", l, 3 * h + ("dk", "dv", "dq").index(kind) - 2))
                    j = 3 * h + ("dk", "dv", "dq").index(kind)
                    if n == TOK:
                        act.activation(pad3[i][:, SEQ + 2:TOK + 2], place[u][:, SEQ:TOK], ACT.Copy).then_inc(*tick("act", "p3c", l, j))
                    act.activation(pad3[i][:, 1:SEQ + 1], place[u][:, 0:SEQ], ACT.Copy).then_inc(*tick_read("act", u))
                    act.wait_ge(*done("c3", l, j))
                    if l:
                        act.wait_ge(*done("xw", l - 1, KT - 1))
                    if kind == "dv":
                        dst = vb[h % 2]
                        if h >= 2:
                            act.wait_ge(*done("pe", ("vturn", l, h - 2)))
                    else:
                        dst = (qT if kind == "dq" else kT)[:, h, :]
                    if n == TOK:
                        act.activation(dst[:, SEQ:TOK], c3[i][:, SEQ + 1:TOK + 1], ACT.Silu).then_inc(*tick("act", "silc", l, j))
                    act.activation(dst[:, 0:SEQ], c3[i][:, 0:SEQ], ACT.Silu).then_inc(*tick("act", "silu", kind, l, h))
                    if kind == "dv":
                        key = ("vturn", l, h)
                        act.wait_ge(*done("pe", key))
                        act.activation(Vtm[:, :, h, :], place[key][:, 0:TOK].rearrange("p (c e) -> p c e", c=NC),
                                            ACT.Copy).then_inc(*tick_read("act", key))
                elif k == "dsum":
                    h = it[2]
                    for i, kind in enumerate(("dk", "dq")):
                        if h:
                            act.wait_ge(*done("dn", kind, l, h - 1))
                        rsqrt(None, rsd[i], 1.0, eps, ("rsd", kind, l, h), ("dss", kind, l, h), ntok(l, kind))
                elif k == "dturn":
                    h = it[2]
                    key = ("kturn", l, h)
                    act.wait_ge(*done("pe", key))
                    act.activation(Ktm[:, :, h, :], place[key][:, 0:TOK].rearrange("p (c e) -> p c e", c=NC),
                                   ACT.Copy).then_inc(*tick_read("act", key))
                elif k == "prep":
                    s = it[2]
                    if s == 0:
                        decay(l, s)
                    for lv in range(LEVELS):
                        if lv > 0:
                            for d in range(2):
                                key = ("T1", l, s, d, lv)
                                act.wait_ge(*done("pe", key))
                                if lv == 1:
                                    act.wait_ge(*done("intra", l, s, d))
                                    act.wait_ge(*done("AT", l, s, d))
                                    act.wait_ge(*done("last", l, s, d))
                                else:
                                    act.wait_ge(*done("pe", ("PU", l, s, d, lv - 1)))
                                act.activation(db[d]["E"][:, :, :], v4(place[key]), ACT.Copy).then_inc(*tick_read("act", key))
                                got[key] = got[("read", key, 0)]
                        if lv < LEVELS - 1:
                            for d in range(2):
                                key = ("MT", l, s, d, lv)
                                act.wait_ge(*done("pe", key))
                                act.activation(db[d]["vs"][:, :, :], v4(place[key]), ACT.Copy).then_inc(*tick_read("act", key))
                                got[("M", l, s, d, lv)] = got[("read", key, 0)]
                elif k == "scan":
                    if it[2] + 1 < NC:
                        decay(l, it[2] + 1)
                elif k == "dout":
                    h = it[2]
                    n = ntok(l, "dz")
                    u = ("dz", l, h)
                    ahead(u)
                    act.wait_ge(*done("pe", u))
                    act.wait_ge(*done("S", l, NC, 1))
                    if h >= 2:
                        act.wait_ge(*done("y32", 1, l, h - 2))
                    act.activation(do[4 + h % 2][:, 0:n], place[u][:, 0:n], ACT.Silu).then_inc(*tick_read("act", u))
                    rsqrt(None, do[2 + h % 2], 1.0 / P, eps, ("dors", l, h), it, n)
                    act.wait_ge(*done("y32", 1, l, h))
                    act.activation(yH[:, h, 0:n], do[6 + h % 2][:, 0:n], ACT.Copy).then_inc(*tick("act", "yh", 1, l, h))
                elif k == "glu":
                    t = it[2]
                    n = ntok(l, "glu")
                    if t == 0:
                        act.wait_ge(*done("padz", l))
                        act.dma_start(cs[:, :, :], rope).then_inc(*tick("rope_in", "rope_in", l, by=16))
                    ahead(("val", l, t))
                    ahead(("glu", l, t))
                    u = ("glu", l, t)
                    act.wait_ge(*done("pe", u))
                    act.wait_ge(*done("padz", l))
                    if t >= 2:
                        act.wait_ge(*done("glu", l, t - 2))
                    act.activation(gl[t % 2][:, 0:n], place[u][:, 0:n], ACT.Sigmoid).then_inc(*tick_read("act", u))
                elif k == "gate":
                    n_, d = it[2], it[3]
                    n = ntok(l, "gate")
                    u = units_of(it)[0]
                    ahead(u)
                    act.wait_ge(*done("pe", u))
                    if last_sg[d % 2]:
                        act.wait_ge(*done(*last_sg[d % 2]))
                    if n_ == 1 and d < 2:
                        act.wait_ge(*done("glu", l, 3))
                        act.wait_ge(*done("yl", 1, l, 3))
                    last_sg[d % 2] = ("gm", l, n_, d)
                    act.activation(sg[d % 2][:, 0:n], place[u][:, 0:n], ACT.Sigmoid).then_inc(*tick_read("act", u))
                elif k == "branch":
                    ahead(units_of(it)[0])
                elif k == "ln":
                    n = ntok(l, "cz")
                    W = ACCW if n == TOK else SEQ
                    for t in range(NT):
                        act.wait_ge(*done("xc", l, t))
                        if t >= 2:
                            act.wait_ge(*done("pe", ("lnvar", l), t - 2))
                        act.activation(sqc[t % 2][:, 0:W], acc[:, t, 0:W], ACT.Square).then_inc(*tick("act", "sqc", l, t))
                    rsqrt(None, rsc, 1.0 / BW, lneps, ("rsc", l), ("lnvar", l), n)
                elif k == "z":
                    t = it[2]
                    n = ntok(l, "cz")
                    u = ("cz", l, t)
                    ahead(u)
                    act.wait_ge(*done("pe", u))
                    act.wait_ge(*done("rsc", l))
                    if t >= 2:
                        act.wait_ge(*done("y32", 0, l, t - 2))
                    act.activation(zt[t % 2][:, 0:n], place[u][:, 0:n], ACT.Silu).then_inc(*tick_read("act", u))
                    act.wait_ge(*done("xn", l, t))
                    for a, b in segs(n):
                        o = HALO if a else 0
                        act.activation(acc[:, t, a + o:b + o], acc[:, t, a + o:b + o], ACT.Silu,
                                         scale=vecs[:, l, V_LG + t:V_LG + t + 1],
                                         bias=vecs[:, l, V_LB + t:V_LB + t + 1]).then_inc(*tick("act", "lns", l, t, a))
                    act.wait_ge(*done("y32", 0, l, t))
                    act.activation(yH[:, t, 0:n], zt[2 + t % 2][:, 0:n], ACT.Copy).then_inc(*tick("act", "yh", 0, l, t))
                elif k == "qunit":
                    h, kind = it[2], it[3]
                    u = (kind, l, h)
                    n = ntok(l, kind)
                    dst = (qh if kind == "aq" else kh)[h % 2]
                    ahead(u)
                    act.wait_ge(*done("pe", u))
                    if h == 0 and kind == "aq":
                        act.wait_ge(*done("yl", 0, l, NT - 1))
                    if kind == "ak":
                        act.wait_ge(*done("pe", ("ss", "aq", l, h)))
                    elif h:
                        act.wait_ge(*done("pe", ("ss", "ak", l, h - 1)))
                        if h >= 2:
                            act.wait_ge(*done("pe", ("oss", l, h - 2)))
                    act.activation(at1[0][:, 0:n], place[u][:, 0:n], ACT.Square).then_inc(*tick("act", "asq", kind, l, h))
                    if h >= 2:
                        act.wait_ge(*done("pe", ("sc", l, h - 2, ntok(l, "aq") // P - 1, 1)))
                    act.activation(dst[:, 0:n], place[u][:, 0:n], ACT.Copy).then_inc(*tick_read("act", u))
                elif k == "qsum":
                    h, kind = it[2], it[3]
                    if kind == "ak":
                        act.wait_ge(*done("an", "aq", l, h))
                    elif h:
                        act.wait_ge(*done("an", "ak", l, h - 1))
                        if h >= 2:
                            act.wait_ge(*done("ao", l, h - 2))
                    rsqrt(None, at1[1], 1.0 / 64, eps, ("ars", kind, l, h), ("ss", kind, l, h), ntok(l, kind))
                elif k == "vunit":
                    h = it[2]
                    u = ("av", l, h)
                    ahead(u)
                    act.wait_ge(*done("pe", u))
                    if h:
                        act.wait_ge(*done("pe", ("aturn", l, h - 1)))
                    if h >= 2:
                        act.wait_ge(*done("yl", 2, l, h - 2))
                    act.activation(vr[:, :], place[u][:, 0:TOK], ACT.Copy).then_inc(*tick_read("act", u))
                    got[("vr", l, h)] = got[("read", u, 0)]
                elif k == "vturn":
                    h = it[2]
                    key = ("aturn", l, h)
                    act.wait_ge(*done("pe", key))
                    if h >= 2:
                        act.wait_ge(*done("pe", ("o", l, h - 2, ntok(l, "aq") // P - 1)))
                    act.activation(Va[h % 2][:, :, :].rearrange("p c e -> p (c e)"), place[key][:, 0:TOK],
                                   ACT.Copy).then_inc(*tick_read("act", key))
                    got[("Va", l, h)] = got[("read", key, 0)]
                elif k == "att":
                    h, qt = it[2], it[3]
                    nq = ntok(l, "aq") // P
                    if qt == 0:
                        soft(l, h, 0)
                    if qt + 1 < nq:
                        soft(l, h, qt + 1)
                    w = TOK if qt < 4 else CTX
                    key = ("pt", l, h, qt)
                    act.wait_ge(*done("pe", key))
                    if qt >= 2:
                        act.wait_ge(*done("pe", ("o", l, h, qt - 2)))
                    elif h:
                        act.wait_ge(*done("pe", ("o", l, h - 1, nq - 2 + qt % 2)))
                    act.activation(aT[qt % 2][:, :, :].rearrange("p c e -> p (c e)")[:, 0:w],
                                   place[key][:, 0:w], ACT.Copy).then_inc(*tick_read("act", key))
                    got[("aT", l, h, qt)] = got[("read", key, 0)]
                elif k == "aout":
                    h = it[2]
                    n = ntok(l, "az")
                    u = ("az", l, h)
                    ahead(u)
                    act.wait_ge(*done("ocopy", l, h, n // P - 1))
                    act.wait_ge(*done("pe", ("ss", "ak", l, min(h + 1, 3))))
                    if h:
                        act.wait_ge(*done("pe", ("oss", l, h - 1)))
                        act.wait_ge(*done("ao", l, h - 1))
                        act.wait_ge(*done("yl", 2, l, h - 1))
                    act.activation(at1[0][:, 0:n], at1[2][:, 0:n], ACT.Square).then_inc(*tick("act", "aosq", l, h))
                    act.wait_ge(*done("an", "ak", l, min(h + 1, 3)))
                    act.wait_ge(*done("pe", ("aturn", l, min(h + 1, 3))))
                    rsqrt(None, at1[1], 1.0 / P, eps, ("aors", l, h), ("oss", l, h), n)
                    act.wait_ge(*done("pe", u))
                    act.activation(vr[:, 0:n], place[u][:, 0:n], ACT.Silu).then_inc(*tick_read("act", u))
                    act.wait_ge(*done("y32", 2, l, h))
                    act.activation(yH[:, h, 0:n], vr[:, 0:n], ACT.Copy).then_inc(*tick("act", "yh", 2, l, h))
                elif k == "out":
                    n = ntok(l, "wout")
                    act.wait_ge(*done("pe", ("branch2", l, 3)))
                    act.dma_start(xs[:, :, 0:n], xT[:, :, 0:n] if l == 0 else xscr[:, :, 0:n]).then_inc(*tick("x_in", "x_back", l, by=16))
                    for t in range(KT):
                        act.wait_ge(*done("gadd", l, 2, t))
                        act.activation(hH[:, t, 0:n], mT[:, t, 0:n], ACT.Copy).then_inc(*tick("act", "mH", l, t))
                    for d, u in enumerate(units_of(it)):
                        ahead(u)
                        act.wait_ge(*done("xnew", l, d))
                        dst = xscr[:, d, :] if l < DEPTH - 1 else outT[:, d, :]
                        act.dma_start(dst, xs[:, d, 0:n]).then_inc(*tick("x_out", "xw", l, d, by=16))
            act.wait_ge(*done("xw", DEPTH - 1, KT - 1))

        @block.vector
        def _(dve):
            stage[0] = "start"
            def col(l, c, rows=P):
                return vecs[0:rows, l, c:c + 1]

            dve.wait_ge(*done("con_in"))
            dve.wait_ge(*done("misc"))
            for l in range(DEPTH):
                for j in range(2):
                    dve.tensor_tensor(lamp[:, l, j, :], lamt[:, l, 2 * j, :], lamt[:, l, 2 * j + 1, :], ALU.mult).then_inc(*tick("dve", "lamp", l, j))
            dve.wait_ge(*done("lamp", 1, 1))
            dve.tensor_reduce(lam_dot[:, :, :], lamp[:, :, :, :], AX_X, ALU.add).then_inc(*tick("dve", "lamdot"))
            dve.wait_ge(*done("cs32"))
            dve.wait_ge(*done("csH"))
            dve.tensor_tensor(csx4[:, :, 2:4], cs32[:, :, :], csx4[:, :, 0:2].bitcast(F32), ALU.subtract).then_inc(*tick("dve", "csL_"))
            got[("csL",)] = got[("csL_",)]
            for l in range(DEPTH):
                lam0 = 0.8 - 0.6 * math.exp(-0.3 * l)
                dve.tensor_scalar(qg8[:, l:l + 1], col(l, V_QG), 64 ** -0.5, None, ALU.mult).then_inc(*tick("dve", "qg8", l))
                dve.tensor_scalar(sub1[:, l:l + 1], col(l, V_SUB), 1.0 - lam0, None, ALU.mult).then_inc(*tick("dve", "sub1", l))
                dve.wait_ge(*done("aexp", l))
                dve.tensor_scalar(nega[:, l:l + 1], nega[:, l:l + 1], -1.0, None, ALU.mult).then_inc(*tick("dve", "nega", l))
                dve.wait_ge(*done("lamexp"))
                dve.tensor_tensor(nlam[:, l:l + 1], lam_exp[:, l, 1:2], lam_exp[:, l, 0:1], ALU.subtract).then_inc(*tick("dve", "nl0", l))
                dve.wait_ge(*done("nl0", l))
                dve.tensor_scalar(nlam[:, l:l + 1], nlam[:, l:l + 1], -lam0, None, ALU.add).then_inc(*tick("dve", "nlam", l))

            done_lo = [0]

            def ahead(u):
                while done_lo[0] < min(WIDX[u] + 3, len(UNITS)):
                    w = done_lo[0]
                    v = UNITS[w]
                    done_lo[0] += 1
                    if low_on_vector(v):
                        dve.wait_ge(*done("hi", v))
                        dve.tensor_tensor(wL[w % 3][:, :], raw[w % 3][:, :], wH[w % 3][:, :].bitcast(F32),
                                          ALU.subtract).then_inc(*tick("dve", "lo", v))

            def ada_col(l, m):
                key = ("adaT", l, m)
                if key in added:
                    return
                added.add(key)
                dve.wait_ge(*done("pe", key))
                dve.tensor_scalar(ada[:, l, m, :], place[key][:, 0:2], col(l, V_BADA + m), None,
                                  ALU.add).then_inc(*tick("dve", "ada0", l, m))
                dve.wait_ge(*done("ada0", l, m))
                dve.tensor_tensor(ada[:, l, m, :], ada[:, l, m, :], place[key][:, 2:4],
                                  ALU.add).then_inc(*tick_read("dve", key))
                got[("ada", l, m)] = got[("read", key, 0)]

            def maxes(l, h, qt):
                w = TOK if qt < 4 else CTX
                i = qt % 2
                for m in range(2):
                    key = ("sc", l, h, qt, m)
                    dve.wait_ge(*done("pe", key))
                    dve.tensor_reduce(stat[:, i, m:m + 1], place[key][:, 0:w], AX_X,
                                      ALU.max).then_inc(*tick("dve", "mx", l, h, qt, m))
                dve.wait_ge(*done("mx", l, h, qt, 1))
                dve.tensor_scalar(stat[:, i, 2:4], stat[:, i, 0:2], -1.0, None,
                                  ALU.mult).then_inc(*tick("dve", "nmx", l, h, qt))

            def decay(l, s):
                for d in range(2):
                    b = db[d]
                    g = ("G", l, s, d)
                    dve.wait_ge(*done("read", g, 0))
                    dve.wait_ge(*done("gcol", l))
                    if s:
                        dve.wait_ge(*done("pe", ("PU", l, s - 1, d, LEVELS - 1)))
                    else:
                        dve.wait_ge(*done("prepfree", l))
                    for h in range(NT):
                        c = 8 + 4 * d + h
                        ins = dve.scalar_tensor_tensor(b["E"][:, h, :], place[g][:, h * P:(h + 1) * P],
                                                       gcol[:, d, ORDER[d][s], c:c + 1], neg(d), ALU.subtract, ALU.add)
                    ins.then_inc(*tick_read("dve", g))
                    got[("E", l, s, d)] = got[("read", g, readers[g] - 1)]

            added = set()
            last_gm = [None]
            conv_done = [0]

            def conv(l, n):
                W = ACCW if ntok(l, "val") == TOK else SEQ
                for _ in range(n):
                    if conv_done[0] >= 2 * CK:
                        return
                    pr, k = divmod(conv_done[0], CK)
                    conv_done[0] += 1
                    for t in (2 * pr, 2 * pr + 1):
                        w = col(l, V_CW + t * CK + k)
                        if k == 0:
                            dve.wait_ge(*done("glu", l, t))
                            ins = dve.tensor_scalar(acc[:, t, 0:W], padc[:, t, 0:W], w, col(l, V_CB + t),
                                                    ALU.mult, ALU.add)
                        else:
                            dve.wait_ge(*done("tap", l, t, k - 1))
                            ins = dve.scalar_tensor_tensor(acc[:, t, 0:W], padc[:, t, k:k + W], w, acc[:, t, 0:W],
                                                           ALU.mult, ALU.add)
                        ins.then_inc(*tick("dve", "tap", l, t, k))
                        if k == CK - 1:
                            got[("conv", l, t)] = got[("tap", l, t, k)]

            for it in ITEMS:
                stage[0], k, l = it[0], it[0], it[1]
                if k == "ada":
                    m = it[2]
                    ahead(("ada", l, m))
                    if m:
                        ada_col(l, m - 1)
                    elif l:
                        ada_col(0, 23)
                    if m == (15 if l == 0 else 23):
                        ada_col(l, m)
                    if m == (15 if l == 0 else 23):
                        dve.wait_ge(*done("ada", l, 15))
                        dve.scalar_tensor_tensor(gs[:, l, :, :], ada[:, l, 8:16, :], 1.0,
                                                 bc(vecs[:, l, V_NG:V_NG + KT], 2), ALU.add,
                                                 ALU.mult).then_inc(*tick("dve", "gs", l))
                elif k == "nh":
                    dve.wait_ge(*done("gs", l))
                    dve.wait_ge(*done("rsn", l))
                    if l:
                        dve.wait_ge(*done("pe", ("wout", l - 1, KT - 1)))
                    for t in range(KT):
                        for p, (a, b) in enumerate(segs(TOK)):
                            if t >= 2:
                                dve.wait_ge(*done("h", l, t - 2))
                                dve.wait_ge(*done("hH", l, t - 2, p))
                            dve.scalar_tensor_tensor(hn[t % 2][:, a:b], xs[:, t, a:b], gs[:, l, t, p:p + 1],
                                                       rsn[:, a:b], ALU.mult, ALU.mult).then_inc(*tick("dve", "hn", l, t, p))
                        if t:
                            lowh(l, t - 1)
                    lowh(l, KT - 1)
                elif k == "gb":
                    dve.wait_ge(*done("gln", l))
                    dve.wait_ge(*done("rm", l))
                    dve.wait_ge(*done("nega", l))
                    dve.scalar_tensor_tensor(gbt[1][:, :], gbt[1][:, :], 0.0, gbt[2][:, :], ALU.max,
                                             ALU.add).then_inc(*tick("dve", "sp", l))
                    dve.wait_ge(*done("sp", l))
                    dve.tensor_scalar(gbt[1][:, :], gbt[1][:, :], nega[0:16, l:l + 1], None,
                                      ALU.mult).then_inc(*tick("dve", "g", l))
                    dve.wait_ge(*done("g", l))
                    dve.tensor_tensor_scan(GR[0:16, :], gbt[3][:, :], gbt[1][:, :], 0.0, ALU.mult,
                                           ALU.add).then_inc(*tick("dve", "cum", l, 0))
                    dve.tensor_tensor_scan(GR[32:48, ::-1], gbt[3][:, :], gbt[1][:, ::-1], 0.0, ALU.mult,
                                           ALU.add).then_inc(*tick("dve", "cum", l, 1))
                elif k == "gturn":
                    key = ("gturn", l)
                    dve.wait_ge(*done("pe", key))
                    for d in range(2):
                        dve.tensor_copy(gcol[:, d, :, :].rearrange("p c x -> p (c x)"),
                                        place[key][:, 512 * d:512 * d + NC * 16]).then_inc(*tick("dve", "gcol", l))
                    dve.tensor_copy(bcol[:, :, :].rearrange("p c x -> p (c x)"),
                                    place[key][:, NC * 16:2 * NC * 16]).then_inc(*tick_read("dve", key))
                    got[("bcol", l)] = got[("read", key, 0)]
                elif k == "dqkv":
                    h, kind = it[2], it[3]
                    j = 3 * h + ("dk", "dv", "dq").index(kind)
                    i = j % 2
                    n = ntok(l, kind)
                    W = TOK + 1 if n == TOK else SEQ
                    w0 = V_DW + 3 * (NT * ("dq", "dk", "dv").index(kind) + h)
                    dve.wait_ge(*done("read", (kind, l, h), 0))
                    if n == TOK:
                        dve.wait_ge(*done("p3c", l, j))
                    if j >= 2:
                        ok, oh = ("dk", "dv", "dq")[(j - 2) % 3], (j - 2) // 3
                        dve.wait_ge(*done("silu", ok, l, oh))
                    dve.tensor_scalar(c3[i][:, 0:W], pad3[i][:, 0:W], col(l, w0), None, ALU.mult).then_inc(*tick("dve", "c3a", l, j))
                    dve.wait_ge(*done("c3a", l, j))
                    dve.scalar_tensor_tensor(c3[i][:, 0:W], pad3[i][:, 1:1 + W], col(l, w0 + 1), c3[i][:, 0:W],
                                               ALU.mult, ALU.add).then_inc(*tick("dve", "c3b", l, j))
                    dve.wait_ge(*done("c3b", l, j))
                    dve.scalar_tensor_tensor(c3[i][:, 0:W], pad3[i][:, 2:2 + W], col(l, w0 + 2), c3[i][:, 0:W],
                                               ALU.mult, ALU.add).then_inc(*tick("dve", "c3", l, j))
                elif k == "dsum":
                    h = it[2]
                    for i, kind in enumerate(("dk", "dq")):
                        n = ntok(l, kind)
                        dst = (qT if kind == "dq" else kT)[:, h, 0:n]
                        dve.wait_ge(*done("rsd", kind, l, h))
                        dve.scalar_tensor_tensor(dst, dst, P ** -0.5 if kind == "dq" else 1.0, rsd[i][:, 0:n],
                                                 ALU.mult, ALU.mult).then_inc(*tick("dve", "dn", kind, l, h))
                elif k == "prep":
                    s = it[2]
                    live = l == 0 or s >= 2
                    if s == 0:
                        decay(l, s)
                    for d in range(2):
                        b = db[d]
                        key = ("KK", l, s, d)
                        dve.wait_ge(*done("pe", key))
                        dve.wait_ge(*done("DT", l, s, d))
                        dve.wait_ge(*done("bcol", l))
                        if s:
                            dve.wait_ge(*done("X", l, s - 1, d, LEVELS - 1))
                        for h in range(NT):
                            ins = dve.scalar_tensor_tensor(b["AT"][:, h, :], place[key][:, h * P:(h + 1) * P],
                                                           bcol[:, ORDER[d][s], 4 * d + h:4 * d + h + 1],
                                                           b["E"][:, h, :], ALU.mult, ALU.mult)
                        ins.then_inc(*tick_read("dve", key))
                        got[("AT", l, s, d)] = got[("read", key, 0)]
                        dve.wait_ge(*done("AT", l, s, d))
                        if s:
                            dve.wait_ge(*done("pe", ("U", l, s - 1, d)))
                        dve.tensor_tensor(b["vs"][:, :, :], b["AT"][:, :, :], bh(mask(d, 0)), ALU.mult).then_inc(*tick("dve", "X", l, s, d, 0))
                        dve.wait_ge(*done("X", l, s, d, 0))
                        if s:
                            dve.wait_ge(*done("pe", ("Y", l, s - 1, d)))
                        dve.tensor_tensor(b["Pm"][:, :, :], bh(ident), b["vs"][:, :, :], ALU.subtract).then_inc(*tick("dve", "P", l, s, d, 0))
                    for d in range(2):
                        b = db[d]
                        if live:
                            key = ("QK", l, s, d)
                            dve.wait_ge(*done("pe", key))
                            if s and (l == 0 or s - 1 >= 2):
                                dve.wait_ge(*done("pe", ("O", l, s - 1, d)))
                            dve.tensor_tensor(b["intra"][:, :, :], v4(place[key]), b["E"][:, :, :], ALU.mult).then_inc(*tick_read("dve", key))
                            got[("intra", l, s, d)] = got[("read", key, 0)]
                        else:
                            got[("intra", l, s, d)] = got[("AT", l, s, d)]
                    for lv in range(1, LEVELS):
                        for d in range(2):
                            b = db[d]
                            key = ("PU", l, s, d, lv)
                            dve.wait_ge(*done("pe", key))
                            dve.wait_ge(*done("P", l, s, d, lv - 1))
                            if lv == 1:
                                dve.wait_ge(*done("P", l, s, d, 0))
                            dve.wait_ge(*done("pe", ("MT", l, s, d, lv - 1)))
                            new = fresh(b["Pm"][:, :, :], d, lv)
                            dve.tensor_tensor(new, new, place[key][:, 0:256].rearrange("p (b s) -> p b s", s=1 << lv),
                                              ALU.subtract).then_inc(*tick_read("dve", key))
                            got[("P", l, s, d, lv)] = got[("read", key, 0)]
                elif k == "scan":
                    s = it[2]
                    live = l == 0 or s >= 2
                    for d in range(2):
                        b = db[d]
                        ch = ORDER[d][s]
                        key = ("KS", l, s, d)
                        dve.wait_ge(*done("pe", key))
                        dve.wait_ge(*done("read", ("vturn", l, 3), 0))
                        if s:
                            dve.wait_ge(*done("vs", l, s - 1, d))
                            if l == 0 or s - 1 >= 2:
                                dve.wait_ge(*done("pe", ("O", l, s - 1, d)))
                        dve.tensor_tensor(b["vn"][:, :, :], Vtm[:, ch, :, :], v4(place[key]), ALU.subtract).then_inc(*tick_read("dve", key))
                        got[("R", l, s, d)] = got[("read", key, 0)]
                    for d in range(2):
                        b = db[d]
                        key = ("Y", l, s, d)
                        dve.wait_ge(*done("pe", key))
                        dve.wait_ge(*done("bcol", l))
                        dve.tensor_tensor(b["vn"][:, :, :], v4(place[key]),
                                               bc(bcol[:, ORDER[d][s], 4 * d:4 * d + 4]), ALU.mult).then_inc(*tick_read("dve", key))
                        got[("vn", l, s, d)] = got[("read", key, 0)]
                    if s + 1 < NC:
                        decay(l, s + 1)
                    for d in range(2):
                        ch = ORDER[d][s]
                        if live:
                            key = ("O", l, s, d)
                            dst = oT[:, :, ch * P:(ch + 1) * P]
                            other = ORDER[1 - d].index(ch)
                            dve.wait_ge(*done("pe", key))
                            if (other, 1 - d) < (s, d):
                                dve.wait_ge(*done("oT", l, other, 1 - d))
                                ins = dve.tensor_tensor(dst, dst, v4(place[key]), ALU.add)
                            else:
                                ins = dve.tensor_copy(dst, v4(place[key]))
                            ins.then_inc(*tick_read("dve", key))
                            got[("oT", l, s, d)] = got[("read", key, 0)]
                    for d in range(2):
                        b = db[d]
                        key = ("U", l, s, d)
                        dve.wait_ge(*done("pe", key))
                        dve.wait_ge(*done("Se", l, s, d))
                        dve.tensor_tensor(b["S"][:, :, :], b["S"][:, :, :], v4(place[key]), ALU.add).then_inc(*tick_read("dve", key))
                        got[("S", l, s + 1, d)] = got[("read", key, 0)]
                elif k == "dout":
                    h = it[2]
                    n = ntok(l, "dz")
                    dve.wait_ge(*done("dors", l, h))
                    dve.scalar_tensor_tensor(do[8 + h % 2][:, 0:n], oT[:, h, 0:n], col(l, V_DNG), do[2 + h % 2][:, 0:n],
                                               ALU.mult, ALU.mult).then_inc(*tick("dve", "don", l, h))
                    dve.wait_ge(*done("don", l, h))
                    dve.wait_ge(*done("read", ("dz", l, h), 0))
                    if h >= 2:
                        dve.wait_ge(*done("yh", 1, l, h - 2))
                        dve.wait_ge(*done("yl", 1, l, h - 2))
                    dve.tensor_tensor(do[6 + h % 2][:, 0:n], do[8 + h % 2][:, 0:n], do[4 + h % 2][:, 0:n], ALU.mult).then_inc(*tick("dve", "y32", 1, l, h))
                elif k == "glu":
                    t = it[2]
                    n = ntok(l, "glu")
                    dve.wait_ge(*done("read", ("glu", l, t), 0))
                    dve.wait_ge(*done("pe", ("val", l, t)))
                    dve.wait_ge(*done("padz", l))
                    ps = place[("val", l, t)]
                    if n == TOK:
                        o = 2 * HALO + SEQ
                        dve.tensor_tensor(padc[:, t, o:o + CTX], ps[:, SEQ:TOK], gl[t % 2][:, SEQ:TOK], ALU.mult).then_inc(*tick("dve", "gluc", l, t))
                    dve.tensor_tensor(padc[:, t, HALO:HALO + SEQ], ps[:, 0:SEQ], gl[t % 2][:, 0:SEQ], ALU.mult).then_inc(*tick_read("dve", ("val", l, t)))
                    got[("glu", l, t)] = got[("read", ("val", l, t), 0)]
                    if t == 0:
                        conv_done[0] = 0
                    elif t < 3:
                        conv(l, 8)
                elif k == "branch":
                    n_, p = it[2], it[3]
                    n = ntok(l, "gate")
                    for j in range(2):
                        d = 2 * p + j
                        if n_ == 1:
                            conv(l, 7)
                        u = ("branch%d" % n_, l, p)
                        gu = ("gate%d" % n_, l, d)
                        dve.wait_ge(*done("pe", (u, j)))
                        dve.wait_ge(*done("read", gu, 0))
                        if n_ == 1:
                            dst = mT[:, d, 0:n]
                        else:
                            dst = gm[:, 0:n]
                            if last_gm[0]:
                                dve.wait_ge(*done(*last_gm[0]))
                            last_gm[0] = ("gadd", l, n_, d)
                        dve.tensor_tensor(dst, place[(u, j)][:, 0:n], sg[j][:, 0:n],
                                          ALU.mult).then_inc(*tick_read("dve", (u, j)))
                        got[("gm", l, n_, d)] = got[("read", (u, j), 0)]
                        if n_ == 1:
                            got[("gadd", l, 1, d)] = got[("gm", l, n_, d)]
                    if n_ == 1 and p == 3:
                        conv(l, 2 * CK)
                elif k == "ln":
                    n = ntok(l, "cz")
                    key = ("lnsum", l)
                    dve.wait_ge(*done("pe", key))
                    for t in range(NT):
                        dve.wait_ge(*done("tap", l, t, CK - 1))
                        if n == TOK:
                            dve.scalar_tensor_tensor(acc[:, t, SEQ + HALO:ACCW], place[key][:, SEQ:TOK], -1.0 / BW,
                                                       acc[:, t, SEQ + HALO:ACCW], ALU.mult, ALU.add).then_inc(*tick("dve", "xcc", l, t))
                        ins = dve.scalar_tensor_tensor(acc[:, t, 0:SEQ], place[key][:, 0:SEQ], -1.0 / BW,
                                                       acc[:, t, 0:SEQ], ALU.mult, ALU.add)
                        if t == NT - 1:
                            ins.then_inc(*tick_read("dve", key))
                            got[("xc", l, t)] = got[("read", key, 0)]
                        else:
                            ins.then_inc(*tick("dve", "xc", l, t))
                elif k == "z":
                    t = it[2]
                    n = ntok(l, "cz")
                    dve.wait_ge(*done("read", ("cz", l, t), 0))
                    dve.wait_ge(*done("lns", l, t, 0))
                    if t >= 2:
                        dve.wait_ge(*done("yh", 0, l, t - 2))
                        dve.wait_ge(*done("yl", 0, l, t - 2))
                    if n == TOK:
                        dve.wait_ge(*done("lns", l, t, SEQ))
                        dve.tensor_tensor(zt[2 + t % 2][:, SEQ:TOK], acc[:, t, SEQ + HALO:ACCW], zt[t % 2][:, SEQ:TOK],
                                            ALU.mult).then_inc(*tick("dve", "y32c", 0, l, t))
                    dve.tensor_tensor(zt[2 + t % 2][:, 0:SEQ], acc[:, t, 0:SEQ], zt[t % 2][:, 0:SEQ], ALU.mult).then_inc(*tick("dve", "y32", 0, l, t))
                elif k == "qsum":
                    h, kind = it[2], it[3]
                    n = ntok(l, kind)
                    dst = (qh if kind == "aq" else kh)[h % 2]
                    g = qg8[:, l:l + 1] if kind == "aq" else col(l, V_KG)
                    dve.wait_ge(*done("ars", kind, l, h))
                    dve.scalar_tensor_tensor(dst[:, 0:n], dst[:, 0:n], g, at1[1][:, 0:n],
                                             ALU.mult, ALU.mult).then_inc(*tick("dve", "an", kind, l, h))
                elif k == "qrot":
                    h, kind = it[2], it[3]
                    key = ("rot", kind, l, h)
                    dve.wait_ge(*done("pe", key))
                    dve.wait_ge(*done("rope_in", l))
                    if last_gm[0]:
                        dve.wait_ge(*done(*last_gm[0]))
                    last_gm[0] = ("rope", kind, l, h)
                    dve.tensor_tensor(gm[:, 0:SEQ], place[key][:, 0:SEQ], cs[:, 1, :],
                                      ALU.mult).then_inc(*tick_read("dve", key))
                elif k == "att":
                    h, qt = it[2], it[3]
                    nq = ntok(l, "aq") // P
                    if qt == 0:
                        maxes(l, h, 0)
                    w = TOK if qt < 4 else CTX
                    i = qt % 2
                    dve.wait_ge(*done("read", ("sc", l, h, qt, 1), 0))
                    dve.reciprocal(stat[:, i, 6:8], stat[:, i, 4:6]).then_inc(*tick("dve", "rc", l, h, qt))
                    dve.wait_ge(*done("rc", l, h, qt))
                    dve.tensor_scalar(c1[:, i:i + 1], stat[:, i, 7:8], nlam[:, l:l + 1], None,
                                      ALU.mult).then_inc(*tick("dve", "c1", l, h, qt))
                    dve.wait_ge(*done("c1", l, h, qt))
                    dve.tensor_scalar(Pa[i][1][:, 0:w], Pa[i][1][:, 0:w], c1[:, i:i + 1], None,
                                      ALU.mult).then_inc(*tick("dve", "p1", l, h, qt))
                    dve.wait_ge(*done("p1", l, h, qt))
                    dve.scalar_tensor_tensor(Pa[i][0][:, 0:w], Pa[i][0][:, 0:w], stat[:, i, 6:7], Pa[i][1][:, 0:w],
                                             ALU.mult, ALU.add).then_inc(*tick("dve", "mixp", l, h, qt))
                    if qt + 1 < nq:
                        maxes(l, h, qt + 1)
                    if qt:
                        ocopy(l, h, qt - 1)
                    if qt == nq - 1:
                        ocopy(l, h, qt)
                elif k == "aout":
                    h = it[2]
                    n = ntok(l, "az")
                    dve.wait_ge(*done("aors", l, h))
                    dve.wait_ge(*done("ocopy", l, h, n // P - 1))
                    dve.scalar_tensor_tensor(at1[2][:, 0:n], at1[2][:, 0:n], sub1[:, l:l + 1], at1[1][:, 0:n],
                                               ALU.mult, ALU.mult).then_inc(*tick("dve", "aon", l, h))
                    dve.wait_ge(*done("aon", l, h))
                    dve.wait_ge(*done("read", ("az", l, h), 0))
                    dve.tensor_tensor(vr[:, 0:n], at1[2][:, 0:n], vr[:, 0:n], ALU.mult).then_inc(*tick("dve", "y32", 2, l, h))
                    got[("ao", l, h)] = got[("y32", 2, l, h)]
                elif k == "out":
                    n = ntok(l, "wout")
                    for t in range(KT):
                        dve.wait_ge(*done("mH", l, t))
                        dve.wait_ge(*done("gadd", l, 2, t))
                        dve.tensor_tensor(hL[:, t, 0:n], mT[:, t, 0:n], hH[:, t, 0:n].bitcast(F32), ALU.subtract).then_inc(*tick("dve", "m", l, t))
                    for t, u in enumerate(units_of(it)):
                        dve.wait_ge(*done("pe", u))
                        dve.wait_ge(*done("x_back", l))
                        for p, (a, b) in list(enumerate(segs(n)))[::-1]:
                            ins = dve.scalar_tensor_tensor(xs[:, t, a:b], place[u][:, a:b], ada[:, l, 16 + t, p:p + 1],
                                                           xs[:, t, a:b], ALU.mult, ALU.add)
                            if p == 0:
                                ins.then_inc(*tick_read("dve", u))
                            else:
                                ins.then_inc(*tick("dve", "xnc", l, t))
                        got[("xnew", l, t)] = got[("read", u, 0)]

        @block.gpsimd
        def _(pool):
            stage[0] = "start"
            done_lo = [0]

            def ahead(u):
                while done_lo[0] < min(WIDX[u] + 3, len(UNITS)):
                    w = done_lo[0]
                    v = UNITS[w]
                    done_lo[0] += 1
                    if not low_on_vector(v):
                        pool.wait_ge(*done("hi", v))
                        pool.tensor_tensor(wL[w % 3][:, :], raw[w % 3][:, :], wH[w % 3][:, :].bitcast(F32),
                                           ALU.subtract).then_inc(*tick("pool", "lo", v))

            def lowy(n_, l, h, n, y32):
                pool.wait_ge(*done("yh", n_, l, h))
                pool.tensor_tensor(yL[:, h, 0:n], y32[:, 0:n], yH[:, h, 0:n].bitcast(F32), ALU.subtract).then_inc(*tick("pool", "yl", n_, l, h))
                got[("y", n_, l, h)] = got[("yl", n_, l, h)]

            pool.memset(csx[:, KT * 4:].bitcast(F32), 0.0).then_inc(*tick("pool", "csx0"))
            pool.memset(ones[:, :], 1.0).then_inc(*tick("pool", "ones_"))
            pool.memset(misc[:, 0:1], RMS_EPS).then_inc(*tick("pool", "misc0"))
            pool.memset(misc[:, 1:2], LN_EPS).then_inc(*tick("pool", "misc_"))
            got[("ones",)] = got[("misc",)] = got[("misc_",)]

            for it in ITEMS:
                stage[0], k, l = it[0], it[0], it[1]
                if k == "ada":
                    for u in units_of(it):
                        ahead(u)
                elif k == "gb":
                    pool.wait_ge(*done("h", l, KT - 1))
                    pool.memset(gbt[3][:, :], 1.0).then_inc(*tick("pool", "rm1", l))
                    pool.wait_ge(*done("rm1", l))
                    pool.memset(gbt[3][:, ::P], 0.0).then_inc(*tick("pool", "rm", l))
                    for i in range(2):
                        for c in (0, SEQ + 1, TOK + 2):
                            pool.memset(pad3[i][:, c:c + 1], 0.0).then_inc(*tick("pool", "pad0", l))
                    ahead(units_of(it)[0])
                elif k == "dqkv":
                    ahead(units_of(it)[0])
                elif k == "dsq":
                    h = it[2]
                    for i, kind in enumerate(("dk", "dq")):
                        src = (qT if kind == "dq" else kT)[:, h, 0:ntok(l, kind)]
                        pool.wait_ge(*done("silu", kind, l, h))
                        if h:
                            pool.wait_ge(*done("pe", ("dss", kind, l, h - 1)))
                        pool.tensor_tensor(sqd[i][:, 0:ntok(l, kind)], src, src,
                                           ALU.mult).then_inc(*tick("pool", "sqd", kind, l, h))
                elif k == "prep":
                    s = it[2]
                    live = l == 0 or s >= 2
                    if s == 0:
                        pool.wait_ge(*done("dn", "dq", l, 3))
                        pool.wait_ge(*done("dn", "dk", l, 3))
                        pool.wait_ge(*done("read", ("kturn", l, 3), 0))
                        pool.wait_ge(*done("read", ("vturn", l, 3), 0))
                        pool.wait_ge(*done("bcol", l))
                        for d in range(2):
                            pool.memset(db[d]["S"][:, :, :], 0.0).then_inc(*tick("pool", "S", l, 0, d))
                        got[("prepfree", l)] = got[("S", l, 0, 1)]
                    for d in range(2):
                        b = db[d]
                        lc = P - 1 if d == 0 else 0
                        pool.wait_ge(*done("read", ("G", l, s, d), 0))
                        pool.wait_ge(*done("DT", l, s, d))
                        if s:
                            pool.wait_ge(*done("vs", l, s - 1, d))
                            pool.wait_ge(*done("Se", l, s - 1, d))
                        pool.tensor_copy(lastc[:, d, 0, :], b["E"][:, :, lc]).then_inc(*tick("pool", "last0", l, s, d))
                        pool.tensor_copy(lastc[:, d, 1, :], b["EG"][:, :, lc]).then_inc(*tick("pool", "last", l, s, d))
                    for lv in range(1, LEVELS):
                        for d in range(2):
                            b = db[d]
                            if lv > 1:
                                pool.wait_ge(*done("pe", ("T1", l, s, d, lv - 1)))
                            else:
                                pool.wait_ge(*done("AT", l, s, d))
                                if s:
                                    pool.wait_ge(*done("pe", ("T1", l, s - 1, d, LEVELS - 1)))
                            pool.tensor_tensor(b["X"][:, :, :], b["AT"][:, :, :], bh(mask(d, lv)), ALU.mult).then_inc(*tick("pool", "X", l, s, d, lv))
                        if lv < 5:
                            d = (lv - 1) % 2
                            b = db[d]
                            cc = slice(ORDER[d][s] * P, (ORDER[d][s] + 1) * P)
                            if lv < 3:
                                if s:
                                    pool.wait_ge(*done("pe", ("KS", l, s - 1, d)))
                                pool.tensor_tensor(b["Kg"][:, :, :], kT[:, :, cc], b["EG"][:, :, :], ALU.mult).then_inc(*tick("pool", "Kg", l, s, d))
                            elif live:
                                if s and (l == 0 or s - 1 >= 2):
                                    pool.wait_ge(*done("pe", ("O", l, s - 1, d)))
                                pool.tensor_tensor(b["Qg"][:, :, :], qT[:, :, cc], b["EG"][:, :, :], ALU.mult).then_inc(*tick("pool", "Qg", l, s, d))
                            else:
                                got[("Qg", l, s, d)] = got[("Kg", l, s, d)]
                elif k == "scan":
                    s = it[2]
                    live = l == 0 or s >= 2
                    for d in range(2):
                        b = db[d]
                        pool.wait_ge(*done("vn", l, s, d))
                        pool.wait_ge(*done("last", l, s, d))
                        if s:
                            pool.wait_ge(*done("pe", ("U", l, s - 1, d)))
                        pool.tensor_tensor(b["vs"][:, :, :], b["vn"][:, :, :], bc(lastc[:, d, 0, :]), ALU.mult).then_inc(*tick("pool", "vs", l, s, d))
                    for d in range(2):
                        b = db[d]
                        pool.wait_ge(*done("pe", ("O", l, s, d) if live else ("KS", l, s, d)))
                        pool.tensor_tensor(b["S"][:, :, :], b["S"][:, :, :], bc(lastc[:, d, 1, :]), ALU.mult).then_inc(*tick("pool", "Se", l, s, d))
                elif k == "dout":
                    h = it[2]
                    n = ntok(l, "dz")
                    pool.wait_ge(*done("S", l, NC, 0))
                    pool.wait_ge(*done("S", l, NC, 1))
                    if h >= 2:
                        pool.wait_ge(*done("pe", ("dout", l, h - 2)))
                    pool.tensor_tensor(do[h % 2][:, 0:n], oT[:, h, 0:n], oT[:, h, 0:n], ALU.mult).then_inc(*tick("pool", "dosq", l, h))
                    ahead(units_of(it)[0])
                    lowy(1, l, h, n, do[6 + h % 2])
                elif k == "glu":
                    if it[2] == 0:
                        pool.memset(padc[:, :, :], 0.0).then_inc(*tick("pool", "padz", l))
                    for u in units_of(it):
                        ahead(u)
                elif k == "gate":
                    ahead(units_of(it)[0])
                elif k == "branch":
                    n_, p = it[2], it[3]
                    n = ntok(l, "gate")
                    ahead(units_of(it)[0])
                    if n_ != 1:
                        for d in (2 * p, 2 * p + 1):
                            pool.wait_ge(*done("gm", l, n_, d))
                            pool.tensor_tensor(mT[:, d, 0:n], mT[:, d, 0:n], gm[:, 0:n],
                                               ALU.add).then_inc(*tick("pool", "gadd", l, n_, d))
                elif k == "z":
                    t = it[2]
                    n = ntok(l, "cz")
                    ahead(units_of(it)[0])
                    pool.wait_ge(*done("rsc", l))
                    for a, b in segs(n)[::-1]:
                        o = HALO if a else 0
                        pool.tensor_tensor(acc[:, t, a + o:b + o], acc[:, t, a + o:b + o], rsc[:, a:b], ALU.mult).then_inc(*tick("pool", *(("xnc", l, t) if a else ("xn", l, t))))
                    lowy(0, l, t, n, zt[2 + t % 2])
                elif k in ("qunit", "vunit"):
                    ahead(units_of(it)[0])
                elif k == "qrot":
                    h, kind = it[2], it[3]
                    dst = (qh if kind == "aq" else kh)[h % 2]
                    pool.wait_ge(*done("read", ("rot", kind, l, h), 0))
                    pool.tensor_tensor(dst[:, 0:SEQ], dst[:, 0:SEQ], cs[:, 0, :],
                                       ALU.mult).then_inc(*tick("pool", "ropc", kind, l, h))
                    pool.wait_ge(*done("ropc", kind, l, h))
                    pool.tensor_tensor(dst[:, 0:SEQ], dst[:, 0:SEQ], gm[:, 0:SEQ],
                                       ALU.add).then_inc(*tick("pool", "rope", kind, l, h))
                elif k == "aout":
                    ahead(units_of(it)[0])
                    h = it[2]
                    n = ntok(l, "az")
                    lowy(2, l, h, n, vr)
                elif k == "out":
                    for u in units_of(it):
                        ahead(u)


    return got


def _columns(a, n):
    return a.reshape(n, P).T


def layout(inp):
    f = np.float32
    arr = {}
    x = np.concatenate([np.asarray(inp["x"])[0], np.asarray(inp["ctx"])[0]], axis=0)
    arr["xT"] = np.ascontiguousarray(x.T.reshape(KT, P, TOK).transpose(1, 0, 2))
    c = np.stack([np.asarray(inp["c"])[0], np.asarray(inp["c_ctx"])], axis=1)
    arr["cT"] = np.ascontiguousarray(c.reshape(KT, P, 2).transpose(1, 0, 2))
    w_in, w_ada = np.asarray(inp["w_in"]), np.asarray(inp["w_ada"])
    w_br, w_out = np.asarray(inp["w_branch"]), np.asarray(inp["w_out"])
    ws = np.empty((len(UNITS), P, 1024), f)
    for i, u in enumerate(UNITS):
        kind, l, t = u
        if kind.startswith("branch"):
            b = w_br[l, int(kind[-1])][:, 256 * t:256 * t + 256].reshape(NT, P, 256)
        elif kind == "ada":
            b = w_ada[l][:, P * t:P * t + P].reshape(KT, P, P)
        elif kind == "wout":
            b = w_out[l][:, P * t:P * t + P].reshape(KT, P, P)
        else:
            o = IN_COL[kind] + P * t
            b = w_in[l][:, o:o + P].reshape(KT, P, P)
        ws[i] = b.transpose(1, 0, 2).reshape(P, 1024)
    arr["wstream"] = ws
    vec = np.zeros((P, DEPTH, NV), f)
    for l in range(DEPTH):
        g = {k: np.asarray(v)[l] for k, v in inp.items() if k not in ("x", "c", "ctx", "c_ctx")}
        vec[:, l, V_BADA:V_NG] = _columns(g["b_ada"], 24)
        vec[:, l, V_NG:V_CB] = _columns(g["norm_g"], KT)
        vec[:, l, V_CB:V_LG] = _columns(g["conv_b"], NT)
        vec[:, l, V_LG:V_LB] = _columns(g["conv_ln_g"], NT)
        vec[:, l, V_LB:V_CW] = _columns(g["conv_ln_b"], NT)
        for t in range(NT):
            vec[:, l, V_CW + t * CK:V_CW + (t + 1) * CK] = g["conv_w"][:, P * t:P * t + P].T
        for t in range(3 * NT):
            vec[:, l, V_DW + 3 * t:V_DW + 3 * t + 3] = g["dn_conv_w"][:, P * t:P * t + P].T
        vec[:, l, V_DNG] = g["dn_norm_g"]
        vec[0:64, l, V_QG] = vec[64:128, l, V_QG] = g["da_q_norm_g"]
        vec[0:64, l, V_KG] = vec[64:128, l, V_KG] = g["da_k_norm_g"]
        vec[:, l, V_SUB] = g["da_subln_g"]
        vec[8:16, l, V_DT] = g["dn_dt_bias"].reshape(-1)
        vec[8:16, l, V_AL] = g["dn_a_log"].reshape(-1)
    arr["vec"] = vec
    arr["lamr"] = np.ascontiguousarray(np.broadcast_to(np.asarray(inp["da_lambda"])[None], (P, DEPTH, 4, 64)))
    arr.update(shape_constants())
    return arr


def shape_constants():
    i = np.arange(P)
    con = np.zeros((P, NCON), np.float32)
    con[:, C_ID:C_ID + P] = np.eye(P)
    con[:, C_BLK:C_BLK + P] = (i[:, None] // 64) == (i[None, :] // 64)
    for m in range(P):
        if m % 64 < 32:
            con[m + 32, C_ROT + m] = -1.0
        else:
            con[m - 32, C_ROT + m] = 1.0
    con[:, C_NEG:C_NEG + P] = np.where(i[:, None] <= i[None, :], 0.0, -1e30)
    con[:, C_NEG + P:C_NEG + 2 * P] = np.where(i[:, None] >= i[None, :], 0.0, -1e30)
    for lv in range(LEVELS):
        s = 1 << lv
        same = (i[:, None] // (2 * s)) == (i[None, :] // (2 * s))
        low = same & ((i[:, None] // s) % 2 == 0) & ((i[None, :] // s) % 2 == 1)
        con[:, C_MASK + lv * P:C_MASK + (lv + 1) * P] = low
        con[:, C_MASK + (LEVELS + lv) * P:C_MASK + (LEVELS + lv + 1) * P] = low.T
    n_freq = 16
    inv = (np.float32(10000.0) ** (-np.arange(n_freq, dtype=np.float32) / np.float32(n_freq))).astype(np.float32)
    t = np.arange(SEQ)
    row, colm = (t // 64).astype(np.float32), (t % 64).astype(np.float32)
    ang = np.concatenate([row[:, None] * inv, colm[:, None] * inv], axis=-1)
    ang = np.concatenate([ang, ang], axis=-1).T
    ang = np.concatenate([ang, ang], axis=0)
    rope = np.stack([np.cos(ang), np.sin(ang)], axis=1).astype(np.float32)
    return {"con": con, "rope": rope}


_ARGS = ["wstream", "xT", "cT", "vec", "lamr", "con", "rope"]


def kernel(**inputs):
    import concourse.bacc as _bacc
    from concourse import mybir as _mybir
    from concourse.bass_utils import run_bass_kernel_spmd as _run

    arrays = layout(inputs)

    def program(steps):
        nc = _bacc.Bacc("TRN2", target_bir_lowering=False, num_devices=1)
        args = [nc.dram_tensor(n, arrays[n].shape, _mybir.dt.float32, kind="ExternalInput").ap() for n in _ARGS]
        args.append(nc.dram_tensor("outT", (P, KT, SEQ), _mybir.dt.float32, kind="ExternalOutput").ap())
        return nc, build(nc, *args, steps)

    _, steps = program({})
    nc, _ = program(steps)
    r = _run(nc, [arrays], core_ids=[0])
    out = r.results[0]["outT"]
    return np.ascontiguousarray(out.transpose(2, 1, 0)).reshape(1, SEQ, D)
```
